# Optimizing a Trainium2 kernel written in Bass

```python
import jax, jax.numpy as jnp
from jax import lax
import numpy as np

D_MODEL = 1024
BATCH = 1
SEQ = 256
DEPTH = 2

CTX_LEN = 256
GRID_W = 64
N_HEADS = 8
QK_NOPE = 64
QK_ROPE = 32
QK_HEAD = QK_NOPE + QK_ROPE
V_HEAD = 64
Q_LORA = 384
KV_LORA = 256
KV_IN = KV_LORA + QK_ROPE
ROPE_AXIS_DIM = QK_ROPE // 2
ROPE_THETA = 10000.0
Q_BLOCK = 128
POOL_WINDOWS = (2, 4, 8, 16)
POOL_GROUPS = 4
POOL_GROUP = 128
POOL_WIDTH = POOL_GROUPS * POOL_GROUP
AB_IN = Q_LORA + KV_IN + POOL_WIDTH
MIX_OUT = N_HEADS * V_HEAD + POOL_WIDTH
D_CONV = 1024
CONV_WIDTH = 3
PEER_HEADS = 8
PEER_N_KEYS = 128
PEER_TOPK = 16
PEER_D_KEY = 128
PEER_N_EXPERTS = PEER_N_KEYS * PEER_N_KEYS
PEER_CHUNK = 128
EPS = 1e-6
N_EVEN = (DEPTH + 1) // 2
N_ODD = DEPTH // 2

kernel_name = 'hybrid_mla_pool_shortconv_peer'

def rmsnorm(x, g):
    xf = x.astype(jnp.float32)
    y = xf * lax.rsqrt(jnp.mean(xf * xf, axis=-1, keepdims=True) + EPS)
    return (y * g.astype(jnp.float32)).astype(x.dtype)

def modulate(xn, shift, scale):
    return xn * (1 + scale) + shift

def axial_rope_tables(L):
    rows = L // GRID_W
    row = jnp.broadcast_to(jnp.arange(rows, dtype=jnp.float32)[:, None], (rows, GRID_W)).reshape(-1)
    col = jnp.broadcast_to(jnp.arange(GRID_W, dtype=jnp.float32)[None, :], (rows, GRID_W)).reshape(-1)
    inv = ROPE_THETA ** (-jnp.arange(0, ROPE_AXIS_DIM, 2, dtype=jnp.float32) / ROPE_AXIS_DIM)
    ang = jnp.stack([row[:, None] * inv, col[:, None] * inv], axis=1)
    return jnp.cos(ang), jnp.sin(ang)

def apply_axial_rope(x, cos, sin):
    half = ROPE_AXIS_DIM // 2
    xs = x.reshape(x.shape[:-1] + (2, 2, half))
    x1, x2 = xs[..., 0, :], xs[..., 1, :]
    cs = cos[:, None].astype(x.dtype)
    sn = sin[:, None].astype(x.dtype)
    out = jnp.stack([x1 * cs - x2 * sn, x2 * cs + x1 * sn], axis=-2)
    return out.reshape(x.shape)

def rope_heads(t, cos, sin):
    return jnp.concatenate([t[..., :QK_NOPE], apply_axial_rope(t[..., QK_NOPE:], cos, sin)], axis=-1)

def mla_queries(h_q, q_a_norm, q_b_w, q_norm):
    B, L = h_q.shape[:2]
    q = (rmsnorm(h_q, q_a_norm) @ q_b_w).reshape(B, L, N_HEADS, QK_HEAD)
    return rmsnorm(q, q_norm)

def mla_keys_values(h_kv, kv_a_norm, kv_b_w, k_norm):
    B, L = h_kv.shape[:2]
    ckv, k_rope = h_kv[..., :KV_LORA], h_kv[..., KV_LORA:]
    kv = (rmsnorm(ckv, kv_a_norm) @ kv_b_w).reshape(B, L, N_HEADS, QK_NOPE + V_HEAD)
    k_nope, v = kv[..., :QK_NOPE], kv[..., QK_NOPE:]
    k_r = jnp.broadcast_to(k_rope[:, :, None, :], (B, L, N_HEADS, QK_ROPE))
    k = jnp.concatenate([k_nope, k_r], axis=-1)
    return rmsnorm(k, k_norm), v

def block_attention(q, k, v):
    B, L, H, Dh = q.shape
    nb = L // Q_BLOCK
    qb = q.reshape(B, nb, Q_BLOCK, H, Dh).transpose(1, 0, 2, 3, 4)
    scale = Dh ** -0.5

    def one_block(qi):
        s = jnp.einsum('bqhd,bkhd->bhqk', qi, k).astype(jnp.float32) * scale
        p = jax.nn.softmax(s, axis=-1)
        return jnp.einsum('bhqk,bkhv->bqhv', p.astype(v.dtype), v)

    o = lax.map(one_block, qb)
    return o.transpose(1, 0, 2, 3, 4).reshape(B, L, H * v.shape[-1])

def multiscale_pool(h, pool_w, pool_scale):
    B, L, _ = h.shape
    hf = h.astype(jnp.float32).reshape(B, L, POOL_GROUPS, POOL_GROUP)
    cs = jnp.concatenate([jnp.zeros((B, 1, POOL_GROUPS, POOL_GROUP), jnp.float32), jnp.cumsum(hf, axis=1)], axis=1)
    pos = jnp.arange(L)
    outs = []
    for gi, w in enumerate(POOL_WINDOWS):
        lo = jnp.clip(pos - w // 2, 0, L)
        hi = jnp.clip(pos + w - w // 2, 0, L)
        cnt = (hi - lo).astype(jnp.float32)[None, :, None]
        csg = cs[:, :, gi]
        window_sum = jnp.take(csg, hi, axis=1) - jnp.take(csg, lo, axis=1)
        outs.append(window_sum / cnt - hf[:, :, gi])
    pooled = jnp.stack(outs, axis=2).astype(h.dtype)
    y = jnp.einsum('blgc,gcd->blgd', pooled, pool_w).reshape(B, L, POOL_WIDTH)
    return y * pool_scale

def even_mixer(xm, xmc, update_ctx, cos, sin, w_in, q_a_norm, q_b_w, kv_a_norm, kv_b_w,
               q_norm, k_norm, pool_w, pool_scale, w_out):
    h = xm @ w_in
    h_q, h_kv, h_pool = h[..., :Q_LORA], h[..., Q_LORA:Q_LORA + KV_IN], h[..., Q_LORA + KV_IN:]
    k_c, v_c = mla_keys_values(xmc @ w_in[:, Q_LORA:Q_LORA + KV_IN], kv_a_norm, kv_b_w, k_norm)
    q = rope_heads(mla_queries(h_q, q_a_norm, q_b_w, q_norm), cos, sin)
    k, v = mla_keys_values(h_kv, kv_a_norm, kv_b_w, k_norm)
    k = rope_heads(k, cos, sin)
    attn = block_attention(q, jnp.concatenate([k_c, k], axis=1), jnp.concatenate([v_c, v], axis=1))
    y = jnp.concatenate([attn, multiscale_pool(h_pool, pool_w, pool_scale)], axis=-1) @ w_out
    y_c = None
    if update_ctx:
        q_c = mla_queries(xmc @ w_in[:, :Q_LORA], q_a_norm, q_b_w, q_norm)
        attn_c = block_attention(q_c, k_c, v_c)
        pool_c = multiscale_pool(xmc @ w_in[:, Q_LORA + KV_IN:], pool_w, pool_scale)
        y_c = jnp.concatenate([attn_c, pool_c], axis=-1) @ w_out
    return y, y_c

def short_conv_mixer(xm, w_in, conv_w, w_out):
    h = xm @ w_in
    bg, cg, hv = h[..., :D_CONV], h[..., D_CONV:2 * D_CONV], h[..., 2 * D_CONV:]
    u = cg * hv
    L = u.shape[1]
    up = jnp.pad(u, ((0, 0), (1, 1), (0, 0)))
    conv = up[:, 0:L] * conv_w[0] + up[:, 1:L + 1] * conv_w[1] + up[:, 2:L + 2] * conv_w[2]
    return (bg * conv) @ w_out

def peer_ffn(xm, wq, keys, u_tab, v_tab):
    B, L, D = xm.shape
    xt = xm.reshape(-1, PEER_CHUNK, D)
    half = PEER_D_KEY // 2
    n_cand = PEER_TOPK * PEER_TOPK

    def chunk(xc):
        q = (xc @ wq).reshape(PEER_CHUNK, PEER_HEADS, PEER_D_KEY)
        s1 = jnp.einsum('chd,hkd->chk', q[..., :half], keys[:, 0]).astype(jnp.float32)
        s2 = jnp.einsum('chd,hkd->chk', q[..., half:], keys[:, 1]).astype(jnp.float32)
        v1, i1 = lax.top_k(s1, PEER_TOPK)
        v2, i2 = lax.top_k(s2, PEER_TOPK)
        cand = (v1[..., :, None] + v2[..., None, :]).reshape(PEER_CHUNK, PEER_HEADS, n_cand)
        cid = (i1[..., :, None] * PEER_N_KEYS + i2[..., None, :]).reshape(PEER_CHUNK, PEER_HEADS, n_cand)
        top, pos = lax.top_k(cand, PEER_TOPK)
        eid = jnp.take_along_axis(cid, pos, axis=-1).reshape(PEER_CHUNK, PEER_HEADS * PEER_TOPK)
        g = jax.nn.softmax(top, axis=-1).reshape(PEER_CHUNK, PEER_HEADS * PEER_TOPK)
        u = jnp.take(u_tab, eid, axis=0)
        a = jax.nn.gelu(jnp.einsum('cd,ced->ce', xc, u), approximate=False)
        coef = (g * a.astype(jnp.float32)).astype(xc.dtype)
        return jnp.einsum('ce,ced->cd', coef, jnp.take(v_tab, eid, axis=0))

    return lax.map(chunk, xt).reshape(B, L, D)

def setup_inputs(seed: int = 0) -> dict:
    key = jax.random.key(seed)
    ks = jax.random.split(key, 26)
    D = D_MODEL

    def nrm(k, shape, std):
        return std * jax.random.normal(k, shape, jnp.float32)

    return {
        'x': nrm(ks[0], (BATCH, SEQ, D), 1.0),
        'c': nrm(ks[1], (BATCH, D), 1.0),
        'ctx': nrm(ks[2], (BATCH, CTX_LEN, D), 1.0),
        'c_ctx': nrm(ks[3], (D,), 1.0),
        'mod_w': nrm(ks[4], (DEPTH, D, 6 * D), 0.5 * D ** -0.5),
        'mod_b': nrm(ks[5], (DEPTH, 6 * D), 0.02),
        'norm_mix': 1.0 + nrm(ks[6], (DEPTH, D), 0.02),
        'norm_ffn': 1.0 + nrm(ks[7], (DEPTH, D), 0.02),
        'ab_w_in': nrm(ks[8], (N_EVEN, D, AB_IN), D ** -0.5),
        'q_a_norm': 1.0 + nrm(ks[9], (N_EVEN, Q_LORA), 0.02),
        'q_b_w': nrm(ks[10], (N_EVEN, Q_LORA, N_HEADS * QK_HEAD), Q_LORA ** -0.5),
        'kv_a_norm': 1.0 + nrm(ks[11], (N_EVEN, KV_LORA), 0.02),
        'kv_b_w': nrm(ks[12], (N_EVEN, KV_LORA, N_HEADS * (QK_NOPE + V_HEAD)), KV_LORA ** -0.5),
        'q_norm': 1.0 + nrm(ks[13], (N_EVEN, QK_HEAD), 0.02),
        'k_norm': 1.0 + nrm(ks[14], (N_EVEN, QK_HEAD), 0.02),
        'pool_w': nrm(ks[15], (N_EVEN, POOL_GROUPS, POOL_GROUP, POOL_GROUP), POOL_GROUP ** -0.5),
        'pool_scale': 1.0 + nrm(ks[16], (N_EVEN, POOL_WIDTH), 0.1),
        'ab_w_out': nrm(ks[17], (N_EVEN, MIX_OUT, D), MIX_OUT ** -0.5),
        'c_w_in': nrm(ks[18], (N_ODD, D, 3 * D_CONV), D ** -0.5),
        'c_conv': nrm(ks[19], (N_ODD, CONV_WIDTH, D_CONV), CONV_WIDTH ** -0.5),
        'c_w_out': nrm(ks[20], (N_ODD, D_CONV, D), D_CONV ** -0.5),
        'peer_wq': nrm(ks[21], (DEPTH, D, PEER_HEADS * PEER_D_KEY), D ** -0.5),
        'peer_keys': nrm(ks[22], (DEPTH, PEER_HEADS, 2, PEER_N_KEYS, PEER_D_KEY // 2), (PEER_D_KEY // 2) ** -0.5),
        'peer_u': nrm(ks[23], (DEPTH, PEER_N_EXPERTS, D), D ** -0.5),
        'peer_v': nrm(ks[24], (DEPTH, PEER_N_EXPERTS, D), 1.0),
    }

def reference(x, c, ctx, c_ctx, mod_w, mod_b, norm_mix, norm_ffn, ab_w_in, q_a_norm, q_b_w,
              kv_a_norm, kv_b_w, q_norm, k_norm, pool_w, pool_scale, ab_w_out, c_w_in, c_conv,
              c_w_out, peer_wq, peer_keys, peer_u, peer_v):
    B, L, D = x.shape
    cos, sin = axial_rope_tables(L)
    s_c = jax.nn.silu(c)
    s_cc = jax.nn.silu(c_ctx)
    ctx_s = ctx
    for i in range(DEPTH):
        even = (i % 2 == 0)
        update_ctx = any(j % 2 == 0 for j in range(i + 1, DEPTH))
        need_ctx_in = even or update_ctx
        mod = (s_c @ mod_w[i] + mod_b[i]).reshape(B, 6, D).transpose(1, 0, 2)[:, :, None, :]
        xm = modulate(rmsnorm(x, norm_mix[i]), mod[0], mod[1])
        if need_ctx_in:
            mod_c = (s_cc @ mod_w[i] + mod_b[i]).reshape(6, 1, 1, D)
            xmc = modulate(rmsnorm(ctx_s, norm_mix[i]), mod_c[0], mod_c[1])
        if even:
            e = i // 2
            y, y_c = even_mixer(xm, xmc, update_ctx, cos, sin, ab_w_in[e], q_a_norm[e], q_b_w[e],
                                kv_a_norm[e], kv_b_w[e], q_norm[e], k_norm[e], pool_w[e],
                                pool_scale[e], ab_w_out[e])
        else:
            o = i // 2
            y = short_conv_mixer(xm, c_w_in[o], c_conv[o], c_w_out[o])
            y_c = short_conv_mixer(xmc, c_w_in[o], c_conv[o], c_w_out[o]) if update_ctx else None
        x = x + mod[2] * y
        xf = modulate(rmsnorm(x, norm_ffn[i]), mod[3], mod[4])
        x = x + mod[5] * peer_ffn(xf, peer_wq[i], peer_keys[i], peer_u[i], peer_v[i])
        if update_ctx:
            ctx_s = ctx_s + mod_c[2] * y_c
            xfc = modulate(rmsnorm(ctx_s, norm_ffn[i]), mod_c[3], mod_c[4])
            ctx_s = ctx_s + mod_c[5] * peer_ffn(xfc, peer_wq[i], peer_keys[i], peer_u[i], peer_v[i])
    return x


_drawn_inputs = setup_inputs


def setup_inputs(seed=0):
    import zlib

    import numpy as np

    out = dict(_drawn_inputs(seed))
    spreads = {}
    factors = {'q_a_norm': 7.132, 'kv_a_norm': 4.494, 'q_norm': 8.0, 'k_norm': 6.998}
    for name, (base, spread) in spreads.items():
        noise = np.random.default_rng([zlib.crc32(name.encode()), seed]).standard_normal(out[name].shape)
        drawn = base * np.exp(spread * noise) if base else spread * noise
        out[name] = __import__('jax').numpy.asarray(drawn.astype(out[name].dtype))
    for name, factor in factors.items():
        out[name] = (out[name] * factor).astype(out[name].dtype)
    return out
```

```python
from contextlib import ExitStack

import numpy as np

import concourse.bass as bass
from concourse import mybir

F32 = mybir.dt.float32
U32 = mybir.dt.uint32
ALU = mybir.AluOpType
ACT = mybir.ActivationFunctionType
AX = mybir.AxisListType

P = 128
D = 1024
NC = D // P
T = 256
TT = T // P
HEADS = 8
NOPE, ROPE, VH = 64, 32, 64
QH = NOPE + ROPE
Q_LORA, KV_LORA = 384, 256
QC, KVC = Q_LORA // P, KV_LORA // P
GROUPS = 4
WINDOWS = (2, 4, 8, 16)
PAD = 8
KEYS = 128
TOPK = 16
PICKS = HEADS * TOPK
EPS = 1e-6
LAYERS = 2
MODS = 6
SLOTS = 4
NEG = -3.0e38

STREAM = [("mod", LAYERS * MODS * NC), ("win", 9), ("wout", NC), ("wq0", HEADS), ("u0", KEYS), ("v0", KEYS),
          ("cin", 3 * NC), ("cout", NC), ("wq1", HEADS), ("u1", KEYS), ("v1", KEYS)]
TILE0, _n = {}, 0
for _name, _count in STREAM:
    TILE0[_name] = _n
    _n += _count
COUNT = dict(STREAM)

OUTS = [("win", 9 + 2 + 2), ("qb", HEADS), ("kb", HEADS), ("vb", 4), ("poolw", GROUPS),
        ("wout", NC), ("wq0", HEADS), ("u0", KEYS), ("cin", 3 * NC), ("cout", NC), ("wq1", HEADS), ("u1", KEYS)]
OUT0, _n = {}, 0
for _name, _count in OUTS:
    OUT0[_name] = _n
    _n += _count


def used(name, j):
    if name in SUMS:
        return "tile_used", SUMS[name] + j + 1
    if name == "win":
        j += max(0, min(j - QC + 1, KVC))
    return "out_ready", OUT0[name] + j + 1


SUMS = {"mod": 0, "v0": COUNT["mod"], "v1": COUNT["mod"] + KEYS}


def steps(e, a, b, step):
    return e.Fori(a, b - step + 1, step)


class Chain:

    def __init__(self, eng, sem):
        self.eng, self.sem, self.n, self.at = eng, sem, 0, None

    def value(self):
        return self.n if self.at is None else self.at + self.n

    def inc(self, ins):
        ins.then_inc(self.sem, 1)
        self.n += 1

    def wait(self):
        self.eng.wait_ge(self.sem, self.value())

    def __call__(self, ins):
        self.inc(ins)
        self.wait()

    def enter(self, i, per):
        self.start, self.per, self.at = self.n, per, i * per

    def leave(self, times):
        assert self.n - self.start == self.per
        self.n, self.at = self.start + times * self.per, None


def hybrid_kernel(nc, xT, ctxT, cT, mod_t, mod_b, norms, win_t, wrope, qa_g, kva_g, q_g, k_g, qb_w, kvb_w, pool_w,
                  pool_s, wout_t, cin_t, conv_w, cout_t, wq_t, keys_t, u_t, v_t, ident_c, rot_c, cs_c, cnt_c, out):
    src = {"mod": mod_t, "win": win_t, "wout": wout_t, "wq0": wq_t[0], "wq1": wq_t[1], "u0": u_t[0], "u1": u_t[1],
           "v0": v_t[0], "v1": v_t[1], "cin": cin_t, "cout": cout_t}
    with ExitStack() as ctx:
        def sb(name, shape, dt=F32):
            return ctx.enter_context(nc.sbuf_tensor(name, shape, dt))

        class Sems(dict):
            def __missing__(self, name):
                self[name] = ctx.enter_context(nc.semaphore(name))
                return self[name]

        S = Sems()
        PS = ctx.enter_context(nc.psum_tensor("PS", [P, 8, 512], F32))
        W = [sb(f"W{i}", [P, D]) for i in range(SLOTS)]
        x = sb("x", [P, NC, T])
        xm = sb("xm", [P, NC, T])
        big = sb("big", [P, KEYS * T])
        C = big[:].rearrange("p (k t) -> p k t", t=T)

        at = [0]

        def scratch(n, shape_str=None, **kw):
            a = big[:, at[0]:at[0] + n]
            at[0] += n
            assert at[0] <= KEYS * T
            return a.rearrange(shape_str, **kw) if shape_str else a

        sq = scratch(4096)
        ctx_x = scratch(NC * T, "p (c t) -> p c t", t=T)
        xmc = scratch(NC * T, "p (c t) -> p c t", t=T)
        hq = scratch(QC * T, "p (c t) -> p c t", t=T)
        ckv = scratch(KVC * 2 * T, "p (c t) -> p c t", t=2 * T)
        kro = scratch(2 * T)
        hp = scratch(GROUPS * (T + 2 * PAD), "p (g t) -> p g t", g=GROUPS)
        ws = [scratch(T + 2 * PAD) for _ in range(2)]
        pooled = scratch(GROUPS * T, "p (g t) -> p g t", t=T)
        q_all = scratch(HEADS * T, "p (h t) -> p h t", t=T)
        k_all = scratch(HEADS * 2 * T, "p (h t) -> p h t", t=2 * T)
        v_all = scratch(4 * HEADS * VH, "p (k n) -> p k n", k=4)
        pe2 = scratch(2 * 2 * T, "p (b n) -> p b n", b=2)
        pT = scratch(2 * 4 * T, "p (b k t) -> p b k t", b=2, k=4)
        conv_u = big[:, 4096:4096 + 2 * (T + 2)].rearrange("p (b t) -> p b t", b=2)
        conv_s = big[:, 5120:5120 + T]
        conv_h = big[:, 6144:6144 + 2 * 3 * T].rearrange("p (b k t) -> p b k t", b=2, k=3)
        mix = sb("mix", [P, NC, T])

        rs = sb("rs", [P, 2048])
        small = sb("small", [P, 64])
        eps = sb("eps", [P, 1])
        ones = sb("ones", [P, P])
        zero = sb("zero", [P, P])
        ident = sb("ident", [P, P])
        iota = sb("iota", [P, P])
        sc = sb("sc", [P, NC, 2])
        sct = sb("sct", [P, NC, 2])
        mod = sb("mod", [P, LAYERS * MODS * NC, 2])
        modb = sb("modb", [P, LAYERS * MODS * NC])
        nrm = sb("nrm", [P, 2, LAYERS, NC])
        aff = sb("aff", [P, 5, NC])
        wro = sb("wro", [P, NC, ROPE])
        qag = sb("qag", [P, QC])
        kvag = sb("kvag", [P, KVC])
        qg = sb("qg", [P, 2])
        kg = sb("kg", [P, 1])
        qbw = scratch(QC * HEADS * QH, "p (c n) -> p c n", c=QC)
        kvbw = scratch(KVC * HEADS * P, "p (c n) -> p c n", c=KVC)
        plw = scratch(GROUPS * P, "p (g n) -> p g n", g=GROUPS)
        cnt = scratch(GROUPS * T, "p (g t) -> p g t", g=GROUPS)
        pls = sb("pls", [P, GROUPS])
        cvw = sb("cvw", [P, 3, NC])
        rot = sb("rot", [P, ROPE])
        cs = sb("cs", [P, 2, T])
        keys = sb("keys", [P, HEADS, KEYS])
        sel_v = sb("sel_v", [P, 2, TOPK])
        sel_i = sb("sel_i", [P, 2, HEADS, TOPK], U32)
        sel_f = sb("sel_f", [P, 2, HEADS, TOPK])
        rep = sb("rep", [P, 2 * KEYS])
        cand = sb("cand", [P, TOPK, TOPK])
        top = sb("top", [P, HEADS, TOPK])
        pos = sb("pos", [P, HEADS, TOPK], U32)
        dig = sb("dig", [P, 2, PICKS], U32)
        eq = rs[:].rearrange("p (n j) -> p n j", j=TOPK)
        picks = sb("picks", [P, TT, 3, PICKS])
        picksT = sb("picksT", [P, 3, T])
        oh1 = sb("oh1", [P, 2, 4, KEYS])
        oh2 = sb("oh2", [P, 2, 4, KEYS])
        second = sb("second", [P, 2, 4])

        block = ctx.enter_context(nc.Block())

        def norms_at(k):
            return [(0, 0, 0), (0, 0, 1), (0, 3, 0), (1, 0, 0), (1, 3, 0)][k]

        @block.sync
        def _(e):
            def tile(name, i, j):
                n = TILE0[name] + j
                slot = n % SLOTS
                if not isinstance(i, int):
                    sem, value = used(name, j - SLOTS)
                    e.wait_ge(S[sem], value + i)
                elif n >= SLOTS:
                    before, k = name, j - SLOTS
                    if k < 0:
                        before = names[names.index(name) - 1]
                        k += COUNT[before]
                    sem, value = used(before, k)
                    e.wait_ge(S[sem], value)
                s = src[name][bass.ds(i + j, 1)] if not isinstance(i, int) else src[name][i + j:i + j + 1]
                e.dma_start(W[slot][:], s.rearrange("a p n -> (a p) n")).then_inc(S[f"landed{slot}"], 16)

            def small_loads():
                for dst, s in [(sc[:], cT), (modb[:], mod_b), (nrm[:], norms), (x[:], xT), (ctx_x, ctxT),
                               (ident[:], ident_c)]:
                    e.dma_start(dst, s).then_inc(S["base"], 16)

            def mixer_loads():
                for dst, s in [(wro[:], wrope), (qag[:], qa_g), (kvag[:], kva_g), (qg[0:QH, 0:1], q_g),
                               (kg[0:QH, :], k_g), (qbw, qb_w), (kvbw, kvb_w), (plw, pool_w), (pls[:], pool_s),
                               (cvw[:], conv_w), (rot[NOPE:QH, :], rot_c), (cs[NOPE:QH, :, :], cs_c), (cnt, cnt_c)]:
                    e.dma_start(dst, s).then_inc(S["mixw"], 16)
                e.dma_start(keys[:], keys_t[0]).then_inc(S["keys_landed"], 16)

            names = [name for name, _ in STREAM]
            small_loads()
            for name, count in STREAM:
                i0 = 4
                if name == "cin":
                    e.wait_ge(S["scores_ready"], TT)
                    e.dma_start(keys[:], keys_t[1]).then_inc(S["keys_landed"], 16)
                if count > 12:
                    for j in range(4):
                        tile(name, 0, j)
                    if name == "mod":
                        mixer_loads()
                    with steps(e, 4, count, 4) as i:
                        for j in range(4):
                            tile(name, i, j)
                else:
                    for j in range(count):
                        tile(name, 0, j)
            e.wait_ge(S["x_new"], 4 * NC)
            e.dma_start(out, x[:]).then_inc(S["stored"], 16)
            e.wait_ge(S["stored"], 16)

        @block.gpsimd
        def _(e):
            nc.gpsimd.memset(ones[:], 1.0).then_inc(S["const"], 1)
            nc.gpsimd.memset(zero[:], 0.0).then_inc(S["const"], 1)
            nc.gpsimd.memset(eps[:], EPS).then_inc(S["const"], 1)
            nc.gpsimd.iota(iota[:], [[1, P]], base=0, channel_multiplier=0,
                           allow_small_or_imprecise_dtypes=True).then_inc(S["const"], 1)
            e.wait_ge(S["const"], 4)
            ch = Chain(e, S["pool_chain"])
            for layer in range(LAYERS):
                e.wait_ge(S["picksT"], 6 * (layer + 1))
                with e.Fori(0, T // 8) as i:
                    ch.enter(i, 2)
                    for b in range(2):
                        n0 = layer * (T // 4) + b
                        e.wait_ge(S["g_ready_pad"], 2 * i + n0 + 1)
                        ch.inc(nc.gpsimd.tensor_copy(second[:, b, :], picksT[:, 1, bass.ds(8 * i + 4 * b, 4)]))
                        e.wait_ge(S["const"], 4)
                        ch.wait()
                        for j in range(4):
                            ins = nc.gpsimd.tensor_scalar(oh2[:, b, j, :], iota[:], second[:, b, j:j + 1], None,
                                                          ALU.is_equal)
                        ins.then_inc(S["oh2_ready"], 1)
                    ch.leave(T // 8)

        @block.tensor
        def _(e):
            mm = nc.tensor.matmul

            def landed(name, i, j):
                n = TILE0[name] + j
                e.wait_ge(S[f"landed{n % SLOTS}"], 16 * (n // SLOTS + 1) + 4 * i)
                return W[n % SLOTS]

            def bank_of(name, i, j):
                n = OUT0[name] + j
                if n >= 2 or not isinstance(i, int):
                    e.wait_ge(S["out_taken"], n - 1 + i)
                return n % 2

            def linear(name, i, j, rhs, oj=None, oi=None):
                w = landed(name, i, j)
                b = bank_of(name, i if oi is None else oi, j if oj is None else oj)
                for c in range(NC):
                    ins = mm(PS[:, b, 0:T], w[:, c * P:(c + 1) * P], rhs[:, c, :], start=c == 0, stop=c == NC - 1)
                return ins

            def end(ins):
                ins.then_inc(S["out_ready"], 1)

            def norm(k, width=T, chunks=NC, base=0):
                e.wait_ge(S["norm_sq"], k + 1)
                for c in range(chunks):
                    ins = mm(PS[:, 7, 0:width], ones[:], sq[:, c * width:(c + 1) * width], start=c == 0, stop=c == chunks - 1)
                ins.then_inc(S["norm_ss"], 1)

            e.wait_ge(S["silu"], 1)
            e.wait_ge(S["const"], 4)

            def mod_step(i, j0):
                b = (j0 // 4) % 2
                for j in range(4):
                    w = landed("mod", i * 8 if not isinstance(i, int) else 0, j0 + j)
                    if j == 0 and not (isinstance(i, int) and j0 < 8):
                        e.wait_ge(S["mod_taken"], 2 * i + j0 // 4 - 1)
                    for c in range(NC):
                        ins = mm(PS[:, b, 2 * j:2 * j + 2], w[:, c * P:(c + 1) * P], sc[:, c, :], start=c == 0,
                                 stop=c == NC - 1)
                    ins.then_inc(S["tile_used"], 1)

            mod_step(0, 0)
            mod_step(0, 4)
            with e.Fori(1, COUNT["mod"] // 8) as i:
                mod_step(i, 0)
                mod_step(i, 4)

            norm(0)
            norm(1)
            e.wait_ge(S["norm_out"], 2)
            e.wait_ge(S["mixw"], 13 * 16)
            o = 0
            for j in range(9):
                both = QC <= j < QC + KVC
                if both:
                    w = landed("win", 0, j)
                    b = bank_of("win", 0, o)
                    for c in range(NC):
                        ins = mm(PS[:, b, 0:T], w[:, c * P:(c + 1) * P], xmc[:, c, :], start=c == 0, stop=c == NC - 1)
                    ins.then_inc(S["out_ready"], 1)
                    o += 1
                end(linear("win", 0, j, xm, oj=o))
                o += 1
            for r in (xmc, xm):
                b = bank_of("win", 0, o)
                for c in range(NC):
                    ins = mm(PS[NOPE:QH, b, 0:T], wro[:, c, :], r[:, c, :], start=c == 0, stop=c == NC - 1)
                ins.then_inc(S["out_ready"], 1)
                o += 1
            norm(2, chunks=QC)
            for h in range(HEADS):
                if h == 0:
                    e.wait_ge(S["norm_out"], 3)
                b = bank_of("qb", 0, h)
                for c in range(QC):
                    ins = mm(PS[0:QH, b, 0:T], qbw[:, c, h * QH:(h + 1) * QH], hq[:, c, :], start=c == 0, stop=c == QC - 1)
                ins.then_inc(S["out_ready"], 1)
            norm(3, width=2 * T, chunks=KVC)
            for h in range(HEADS):
                if h == 0:
                    e.wait_ge(S["norm_out"], 4)
                b = bank_of("kb", 0, h)
                for c in range(KVC):
                    ins = mm(PS[0:NOPE, b, :], kvbw[:, c, h * P:h * P + NOPE], ckv[:, c, :], start=c == 0, stop=c == KVC - 1)
                ins.then_inc(S["out_ready"], 1)
            for kc in range(4):
                b = bank_of("vb", 0, kc)
                for c in range(KVC):
                    ins = mm(PS[:, b, :], ckv[:, c, kc * P:(kc + 1) * P],
                             kvbw[:, c, :].rearrange("p (h n) -> p h n", h=HEADS)[:, :, NOPE:], start=c == 0,
                             stop=c == KVC - 1)
                ins.then_inc(S["out_ready"], 1)
            for n in range(3):
                e.wait_ge(S["head_sq"], n + 1)
                if n:
                    e.wait_ge(S["head_rt"], n)
                for j in range(4):
                    ins = mm(PS[0:QH, 2 + j, :], ones[0:QH, 0:QH], sq[0:QH, j * 512:(j + 1) * 512], start=True, stop=True)
                ins.then_inc(S["head_ss"], 1)
            for n, a in enumerate([q_all, k_all]):
                e.wait_ge(S["head_n"], n + 1)
                e.wait_ge(S["head_rt"], 3)
                if n == 1:
                    e.wait_ge(S["roped"], 1)
                for j in range(4):
                    r = a[NOPE:QH, 2 * j:2 * j + 2, :] if n == 0 else a[NOPE:QH, 2 * j:2 * j + 2, T:]
                    ins = mm(PS[NOPE:QH, 2 + j, :], rot[NOPE:QH, :], r, start=True, stop=True)
                ins.then_inc(S["rot"], 1)
            for g in range(GROUPS):
                e.wait_ge(S["pooled"], g + 1)
                b = bank_of("poolw", 0, g)
                mm(PS[:, b, 0:T], plw[:, g, :], pooled[:, g, :], start=True, stop=True).then_inc(S["out_ready"], 1)
            e.wait_ge(S["roped"], 2)

            def scores(k):
                h, t = divmod(k, TT)
                if k >= 2:
                    e.wait_ge(S["att_exp"], k - 1)
                mm(PS[:, 2 + k % 2, :], q_all[0:QH, h, t * P:(t + 1) * P], k_all[0:QH, h, :], start=True,
                   stop=True).then_inc(S["att_s"], 1)

            def turn(k):
                e.wait_ge(S["att_p"], k + 1)
                if k >= 2:
                    e.wait_ge(S["att_c"], k - 1)
                for j in range(4):
                    ins = nc.tensor.transpose(PS[:, 4 + k % 2, j * P:(j + 1) * P], pe2[:, k % 2, j * P:(j + 1) * P], ident[:])
                ins.then_inc(S["att_t"], 1)

            def values(h):
                e.wait_ge(S["att_c"], 2 * h + 2)
                if h >= 2:
                    e.wait_ge(S["att_o"], h - 1)
                lo = h % 2 * VH
                for j in range(4):
                    ins = mm(PS[lo:lo + VH, 6 + h % 2, 0:T], v_all[:, j, h * VH:(h + 1) * VH], pT[:, h % 2, j, :],
                             start=j == 0, stop=j == 3)
                ins.then_inc(S["att_v"], 1)

            scores(0)
            scores(1)
            for k in range(HEADS * TT):
                turn(k)
                if k + 2 < HEADS * TT:
                    scores(k + 2)
                if k % 2 == 1:
                    values(k // 2)
            e.wait_ge(S["att_o"], HEADS)
            e.wait_ge(S["pool_out"], GROUPS)
            for n in range(NC):
                end(linear("wout", 0, n, mix))

            for layer in range(LAYERS):
                if layer == 1:
                    norm(5)
                    e.wait_ge(S["norm_out"], 6)
                    with steps(e, 0, 3 * NC, 12) as i:
                        for j in range(12):
                            end(linear("cin", i, j, xm))
                    e.wait_ge(S["conv_out"], NC)
                    for n in range(NC):
                        end(linear("cout", 0, n, mix))
                norm(4 if layer == 0 else 6)
                e.wait_ge(S["norm_out"], 5 if layer == 0 else 7)
                for h in range(HEADS):
                    end(linear(f"wq{layer}", 0, h, xm))
                e.wait_ge(S["keys_landed"], 16 * (layer + 1))
                u = f"u{layer}"
                for t in range(TT):
                    if t == 0:
                        e.wait_ge(S["queries"], HEADS * (layer + 1))
                    else:
                        e.wait_ge(S["topk_read"], HEADS * (TT * layer + t))
                    for half in range(2):
                        lo = half * 64
                        for h in range(HEADS):
                            ins = mm(PS[:, 2 + 2 * half + h // 4, h % 4 * P:(h % 4 + 1) * P],
                                     mix[lo:lo + 64, h, t * P:(t + 1) * P], keys[lo:lo + 64, h, :], start=True, stop=True)
                    ins.then_inc(S["scores_ready"], 1)
                    with steps(e, t * KEYS // TT, (t + 1) * KEYS // TT, 4) as i:
                        for j in range(4):
                            end(linear(u, i, j, xm))
                for t in range(TT):
                    e.wait_ge(S["picks"], TT * layer + t + 1)
                    for k in range(3):
                        ins = nc.tensor.transpose(PS[:, 6, k * P:(k + 1) * P], picks[:, t, k, :], ident[:])
                    ins.then_inc(S["picks_turned"], 1)
                    e.wait_ge(S["picksT"], 3 * (TT * layer + t + 1))
                with e.Fori(0, T // 8) as i:
                    for b in range(2):
                        n = layer * (T // 4) + b
                        e.wait_ge(S["oh2_ready"], 2 * i + n + 1)
                        e.wait_ge(S["oh1_ready"], 2 * i + n + 1)
                        e.wait_ge(S["g_taken_pad"], 2 * i + n + 1)
                        for j in range(4):
                            ins = mm(PS[:, 6 + b, j * P:(j + 1) * P], oh2[:, b, j, :], oh1[:, b, j, :], start=True, stop=True)
                        ins.then_inc(S["g_ready_pad"], 1)
                e.wait_ge(S["topk_read"], HEADS * TT * (layer + 1))
                e.wait_ge(S["g_taken_pad"], 2 + (layer + 1) * (T // 4))
                for b in range(4):
                    mm(PS[:, 2 + b, :], zero[:], xm[:, 0:2, :], start=True, stop=False, skip_group_check=True)
                v = f"v{layer}"
                with steps(e, 0, KEYS, 4) as i:
                    for j in range(4):
                        w = landed(v, i, j)
                        for c in range(NC):
                            ins = mm(PS[:, 2 + c // 2, c % 2 * T:(c % 2 + 1) * T], w[:, c * P:(c + 1) * P],
                                     C[:, bass.ds(i + j, 1), :], start=False, stop=False, skip_group_check=True)
                        ins.then_inc(S["tile_used"], 1)

        @block.scalar
        def _(e):
            act = nc.scalar.activation
            ch = Chain(e, S["act_chain"])

            def ready(name, i, j):
                n = OUT0[name] + j
                e.wait_ge(S["out_ready"], n + 1 + i)
                return PS[:, n % 2, :]

            def norm(k, a, n, width=T):
                act(sq[:, 0:n], a, ACT.Square).then_inc(S["norm_sq"], 1)
                e.wait_ge(S["norm_ss"], k + 1)
                act(rs[:, 0:width], PS[:, 7, 0:width], ACT.Sqrt, bias=eps[:], scale=width / (n * P)).then_inc(S["norm_rt"], 1)

            e.wait_ge(S["base"], 6 * 16)
            e.wait_ge(S["const"], 4)
            act(sct[:], sc[:], ACT.Exp, scale=-1.0).then_inc(S["cexp"], 1)
            norm(0, x[:], NC * T)
            e.wait_ge(S["norm_rs"], 1)
            norm(1, ctx_x, NC * T)
            o = 0
            for j in range(9):
                if j < QC:
                    act(hq[:, j, :], ready("win", 0, o)[:, 0:T], ACT.Copy).then_inc(S["out_taken"], 1)
                    o += 1
                elif j < QC + KVC:
                    for side in range(2):
                        act(ckv[:, j - QC, side * T:(side + 1) * T], ready("win", 0, o)[:, 0:T], ACT.Copy)\
                            .then_inc(S["out_taken"], 1)
                        o += 1
                else:
                    g = j - QC - KVC
                    e.wait_ge(S["pad_zero"], 1)
                    act(hp[:, g, PAD:PAD + T], ready("win", 0, o)[:, 0:T], ACT.Copy).then_inc(S["out_taken"], 1)
                    o += 1
            for side in range(2):
                act(kro[NOPE:QH, side * T:(side + 1) * T], ready("win", 0, o)[NOPE:QH, 0:T], ACT.Copy)\
                    .then_inc(S["out_taken"], 1)
                o += 1
            e.wait_ge(S["out_taken"], OUT0["qb"])
            norm(2, hq, QC * T)
            for h in range(HEADS):
                act(q_all[0:QH, h, :], ready("qb", 0, h)[0:QH, 0:T], ACT.Copy).then_inc(S["out_taken"], 1)
            norm(3, ckv, KVC * 2 * T, width=2 * T)
            for h in range(HEADS):
                act(k_all[0:NOPE, h, :], ready("kb", 0, h)[0:NOPE, :], ACT.Copy).then_inc(S["out_taken"], 1)
            for kc in range(4):
                act(v_all[:, kc, :], ready("vb", 0, kc), ACT.Copy).then_inc(S["out_taken"], 1)
            e.wait_ge(S["out_taken"], OUT0["poolw"])
            e.wait_ge(S["k_rope"], 1)
            for n in range(3):
                a = q_all[0:QH] if n == 0 else k_all[0:QH, 4 * (n - 1):4 * n, :]
                act(sq[0:QH, 0:2048], a, ACT.Square).then_inc(S["head_sq"], 1)
                e.wait_ge(S["head_ss"], n + 1)
                if n:
                    e.wait_ge(S["head_rs"], n)
                act(rs[0:QH, :], PS[0:QH, 2:6, :], ACT.Sqrt, bias=eps[0:QH, :], scale=1.0 / QH).then_inc(S["head_rt"], 1)
            for g in range(GROUPS):
                act(mix[:, 4 + g, :], ready("poolw", 0, g)[:, 0:T], ACT.Copy, scale=pls[:, g:g + 1])\
                    .then_inc(S["out_taken"], 1)
            e.wait_ge(S["out_taken"], OUT0["wout"])
            e.nop().then_inc(S["pool_out"], GROUPS)

            def exps(k):
                e.wait_ge(S["att_m"], k + 1)
                if k >= 2:
                    e.wait_ge(S["att_t"], k - 1)
                act(pe2[:, k % 2, :], PS[:, 2 + k % 2, :], ACT.Exp, bias=small[:, k:k + 1],
                    accum_out=small[:, 16 + k:17 + k]).then_inc(S["att_exp"], 1)

            exps(0)
            for k in range(HEADS * TT):
                if k + 1 < HEADS * TT:
                    exps(k + 1)
                h, t = divmod(k, TT)
                e.wait_ge(S["att_t"], k + 1)
                if h >= 2:
                    e.wait_ge(S["att_v"], h - 1)
                act(pT[:, h % 2, :, t * P:(t + 1) * P],
                    PS[:, 4 + k % 2, :].rearrange("p (j t) -> p j t", j=4), ACT.Copy).then_inc(S["att_c"], 1)

            for layer in range(LAYERS):
                if layer == 1:
                    e.wait_ge(S["x_new"], 2 * NC)
                    norm(5, x[:], NC * T)
                    with steps(e, 0, 3 * NC, 12) as i:
                        for j in range(12):
                            n, k = divmod(j, 3)
                            if k == 0:
                                e.wait_ge(S["conv_taken"], i // 3 + n + 1)
                            act(conv_h[:, n % 2, k, :], ready("cin", i, j)[:, 0:T], ACT.Copy).then_inc(S["out_taken"], 1)
                k = 4 if layer == 0 else 6
                e.wait_ge(S["x_new"], (2 * layer + 1) * NC)
                norm(k, x[:], NC * T)
                for h in range(HEADS):
                    act(mix[:, h, :], ready(f"wq{layer}", 0, h)[:, 0:T], ACT.Copy).then_inc(S["out_taken"], 1)
                e.wait_ge(S["out_taken"], OUT0[f"wq{layer}"] + HEADS)
                e.nop().then_inc(S["queries"], HEADS)
                for t in range(TT):
                    with steps(e, t * KEYS // TT, (t + 1) * KEYS // TT, 4) as i:
                        for j in range(4):
                            act(C[:, bass.ds(i + j, 1), :], ready(f"u{layer}", i, j)[:, 0:T], ACT.Gelu)\
                                .then_inc(S["out_taken"], 1)
                    e.wait_ge(S["gate_d"], TT * layer + t + 1)
                    act(picks[:, t, 2, :], top[:], ACT.Exp).then_inc(S["gate_e"], 1)
                e.wait_ge(S["out_taken"], OUT0[f"u{layer}"] + KEYS)
                e.nop().then_inc(S["gelu_done"], 1)

        @block.vector
        def _(e):
            v = nc.vector
            ch = Chain(e, S["dve_chain"])
            tt, stt, ts = v.tensor_tensor, v.scalar_tensor_tensor, v.tensor_scalar

            def ready(name, i, j):
                n = OUT0[name] + j
                e.wait_ge(S["out_ready"], n + 1 + i)
                return PS[:, n % 2, :]

            e.wait_ge(S["cexp"], 1)
            ch(ts(sct[:], sct[:], 1.0, None, ALU.add))
            ch(v.reciprocal(sct[:], sct[:]))
            tt(sc[:], sc[:], sct[:], ALU.mult).then_inc(S["silu"], 1)
            v.memset(hp, 0.0).then_inc(S["pad_zero"], 1)
            v.memset(small[:, 63:64], 0.0).then_inc(S["g_ready_pad"], 2)
            v.memset(small[:, 62:63], 0.0).then_inc(S["g_taken_pad"], 2)
            v.memset(small[:, 61:62], 0.0).then_inc(S["conv_taken"], 2)
            with steps(e, 0, COUNT["mod"] // 4, 2) as i:
                for j in range(2):
                    e.wait_ge(S["tile_used"], 4 * i + 4 * j + 4)
                    tt(mod[:, bass.ds(4 * i + 4 * j, 4), :], PS[:, j, 0:8].rearrange("p (a b) -> p a b", b=2),
                       modb[:, bass.ds(4 * i + 4 * j, 4)].unsqueeze(2).broadcast_to([P, 4, 2]), ALU.add)\
                        .then_inc(S["mod_taken"], 1)
            e.wait_ge(S["mod_taken"], COUNT["mod"] // 4)

            def mrow(layer, k, col=0):
                a = layer * MODS * NC + k * NC
                return mod[:, a:a + NC, col:col + 1]

            for k in range(5):
                layer, row, col = norms_at(k)
                ins = stt(aff[:, k, :].unsqueeze(2), mrow(layer, row + 1, col), 1.0,
                          nrm[:, 0 if row == 0 else 1, layer, :].unsqueeze(2), ALU.add, ALU.mult)
            ch(ins)

            def norm(k, src_, dst, which=None, gain=None, chunks=NC, width=T):
                e.wait_ge(S["norm_rt"], k + 1)
                ins = v.reciprocal(rs[:, 0:width], rs[:, 0:width])
                ch(ins)
                for c in range(chunks):
                    if gain is None:
                        layer, row, col = norms_at(which)
                        stt(dst[:, c, :], src_[:, c, :], aff[:, which, c:c + 1], rs[:, 0:width], ALU.mult, ALU.mult)\
                            .then_inc(S["dve_chain"], 1)
                        ch.n += 1
                    else:
                        ins = stt(dst[:, c, :], src_[:, c, :], gain[:, c:c + 1], rs[:, 0:width], ALU.mult, ALU.mult)
                if gain is None:
                    e.wait_ge(S["dve_chain"], ch.n)
                    for c in range(chunks):
                        ins = ts(dst[:, c, :], dst[:, c, :], mrow(layer, row, col)[:, c, :], None, ALU.add)
                ins.then_inc(S["norm_out"], 1)

            norm(0, x, xm, which=0)
            e.wait_ge(S["norm_out"], 1)
            v.memset(small[:, 60:61], 0.0).then_inc(S["norm_rs"], 1)
            norm(1, ctx_x, xmc, which=1)
            e.wait_ge(S["mixw"], 13 * 16)
            ch(ts(qg[0:QH, 1:2], qg[0:QH, 0:1], float(QH) ** -0.5, None, ALU.mult))
            e.wait_ge(S["out_taken"], OUT0["qb"])
            for g, w in enumerate(WINDOWS):
                cur, n, size = hp[:, g, :], T + 2 * PAD, 1
                k = 0
                while size < w:
                    n -= size
                    ch(tt(ws[k % 2][:, 0:n], cur[:, 0:n], cur[:, size:size + n], ALU.add))
                    cur = ws[k % 2]
                    k += 1
                    size *= 2
                a = PAD - w // 2
                ch(tt(pooled[:, g, :], cur[:, a:a + T], cnt[:, g, :], ALU.mult))
                ch(tt(pooled[:, g, :], pooled[:, g, :], hp[:, g, PAD:PAD + T], ALU.subtract))
            e.nop().then_inc(S["pooled"], GROUPS)
            norm(2, hq, hq, gain=qag, chunks=QC)
            norm(3, ckv, ckv, gain=kvag, chunks=KVC, width=2 * T)
            v.tensor_copy(k_all[NOPE:QH], kro[NOPE:QH, :].unsqueeze(1).broadcast_to([ROPE, HEADS, 2 * T]))\
                .then_inc(S["k_rope"], 1)
            for n in range(3):
                e.wait_ge(S["head_rt"], n + 1)
                ch(v.reciprocal(rs[0:QH, :], rs[0:QH, :]))
                a = q_all[0:QH] if n == 0 else k_all[0:QH, 4 * (n - 1):4 * n, :]
                a = a.rearrange("p h t -> p (h t)")
                g = qg[0:QH, 1:2] if n == 0 else kg[0:QH, :]
                ch(stt(a, a, g, rs[0:QH, :], ALU.mult, ALU.mult))
                v.memset(small[:, 60:61], 0.0).then_inc(S["head_rs"], 1)
                if n != 1:
                    e.nop().then_inc(S["head_n"], 1)
            for n, a in enumerate([q_all[NOPE:QH], k_all[NOPE:QH, :, T:]]):
                e.wait_ge(S["rot"], n + 1)
                t2 = rs[NOPE:QH, :].rearrange("p (h t) -> p h t", t=T)
                sin = cs[NOPE:QH, 1, :].unsqueeze(1).broadcast_to([ROPE, HEADS, T])
                cos = cs[NOPE:QH, 0, :].unsqueeze(1).broadcast_to([ROPE, HEADS, T])
                ch(tt(t2, PS[NOPE:QH, 2:6, :].rearrange("p b (h t) -> p (b h) t", t=T), sin, ALU.mult))
                ch(tt(a, a, cos, ALU.mult))
                tt(a, a, t2, ALU.add).then_inc(S["roped"], 1)
                e.wait_ge(S["roped"], n + 1)

            def maxes(k):
                e.wait_ge(S["att_s"], k + 1)
                v.tensor_reduce(small[:, k:k + 1], PS[:, 2 + k % 2, :], AX.X, ALU.max, negate=True).then_inc(S["att_m"], 1)

            maxes(0)
            for k in range(HEADS * TT):
                if k + 1 < HEADS * TT:
                    maxes(k + 1)
                e.wait_ge(S["att_exp"], k + 1)
                ch(v.reciprocal(small[:, 32 + k:33 + k], small[:, 16 + k:17 + k]))
                ts(pe2[:, k % 2, :], pe2[:, k % 2, :], small[:, 32 + k:33 + k], None, ALU.mult).then_inc(S["att_p"], 1)
                if k % 2 == 1 and k >= 3:
                    copy_out = k // 2 - 1
                    e.wait_ge(S["att_v"], copy_out + 1)
                    lo = copy_out % 2 * VH
                    v.tensor_copy(mix[lo:lo + VH, copy_out // 2, :], PS[lo:lo + VH, 6 + copy_out % 2, 0:T])\
                        .then_inc(S["att_o"], 1)
            e.wait_ge(S["att_v"], HEADS)
            v.tensor_copy(mix[VH:, HEADS // 2 - 1, :], PS[VH:, 7, 0:T]).then_inc(S["att_o"], 1)

            def residual(a, layer, row, n):
                return stt(x[:, n, :], a, mrow(layer, row)[:, n, :], x[:, n, :], ALU.mult, ALU.add)

            for n in range(NC):
                residual(ready("wout", 0, n)[:, 0:T], 0, 2, n).then_inc(S["out_taken"], 1)
            e.wait_ge(S["out_taken"], OUT0["wout"] + NC)
            e.nop().then_inc(S["x_new"], NC)

            for layer in range(LAYERS):
                if layer == 1:
                    norm(5, x, xm, which=3)
                    ch(v.memset(conv_u, 0.0))
                    with steps(e, 0, NC, 4) as i:
                        ch.enter(i, 4)
                        for n in range(4):
                            j = n % 2
                            e.wait_ge(S["out_taken"], OUT0["cin"] + 3 * n + 3 + 3 * i)
                            h_ = conv_h[:, j]
                            u_ = conv_u[:, j]
                            ch(tt(u_[:, 1:T + 1], h_[:, 1, :], h_[:, 2, :], ALU.mult))
                            ch(ts(conv_s, u_[:, 0:T], cvw[:, 0, bass.ds(i + n, 1)], None, ALU.mult))
                            ch(stt(conv_s, u_[:, 1:T + 1], cvw[:, 1, bass.ds(i + n, 1)], conv_s, ALU.mult, ALU.add))
                            ch(stt(conv_s, u_[:, 2:T + 2], cvw[:, 2, bass.ds(i + n, 1)], conv_s, ALU.mult, ALU.add))
                            tt(mix[:, bass.ds(i + n, 1), :], h_[:, 0, :], conv_s, ALU.mult).then_inc(S["conv_taken"], 1)
                            e.wait_ge(S["conv_taken"], 2 + n + 1 + i)
                        ch.per = 16
                        ch.leave(NC // 4)
                    e.nop().then_inc(S["conv_out"], NC)
                    for n in range(NC):
                        residual(ready("cout", 0, n)[:, 0:T], 1, 2, n).then_inc(S["out_taken"], 1)
                    e.wait_ge(S["out_taken"], OUT0["cout"] + NC)
                    e.nop().then_inc(S["x_new"], NC)
                norm(4 if layer == 0 else 6, x, xm, which=2 if layer == 0 else 4)
                for t in range(TT):
                    e.wait_ge(S["scores_ready"], TT * layer + t + 1)
                    for h in range(HEADS):
                        for half in range(2):
                            s = PS[:, 2 + 2 * half + h // 4, h % 4 * P:(h % 4 + 1) * P]
                            lo, hi = sel_v[:, half, 0:8], sel_v[:, half, 8:16]
                            ch(v.max(lo, s))
                            v.max_index(sel_i[:, half, h, 0:8], lo, s)
                            ch(v.match_replace(rep[:, 0:KEYS], lo, s, NEG))
                            ch(v.max(hi, rep[:, 0:KEYS]))
                            ch(v.max_index(sel_i[:, half, h, 8:16], hi, rep[:, 0:KEYS]))
                        e.nop().then_inc(S["topk_read"], 1)
                        ch(tt(cand[:], sel_v[:, 0, :].unsqueeze(2).broadcast_to([P, TOPK, TOPK]),
                              sel_v[:, 1, :].unsqueeze(1).broadcast_to([P, TOPK, TOPK]), ALU.add))
                        cd = cand[:].rearrange("p a b -> p (a b)")
                        ch(v.max(top[:, h, 0:8], cd))
                        v.max_index(pos[:, h, 0:8], top[:, h, 0:8], cd)
                        ch(v.match_replace(rep[:], top[:, h, 0:8], cd, NEG))
                        ch(v.max(top[:, h, 8:16], rep[:]))
                        ch(v.max_index(pos[:, h, 8:16], top[:, h, 8:16], rep[:]))
                    ch(v.tensor_copy(sel_f[:], sel_i[:]))
                    pf = pos[:].rearrange("p h k -> p (h k)")
                    ch(ts(dig[:, 0, :], pf, 4, None, ALU.logical_shift_right))
                    ch(ts(dig[:, 1, :], pf, 15, None, ALU.bitwise_and))
                    for half in range(2):
                        ch(tt(eq, dig[:, half, :].unsqueeze(2).broadcast_to([P, PICKS, TOPK]),
                              iota[:, 0:TOPK].unsqueeze(1).broadcast_to([P, PICKS, TOPK]), ALU.is_equal))
                        e4 = eq.rearrange("p (h k) j -> p h k j", h=HEADS)
                        ch(tt(e4, e4, sel_f[:, half].unsqueeze(2).broadcast_to([P, HEADS, TOPK, TOPK]), ALU.mult))
                        ch(v.tensor_reduce(picks[:, t, half, :], eq, AX.X, ALU.add))
                    ch(v.tensor_copy(small[:, 0:8], top[:, :, 0]))
                    tt(top[:], top[:], small[:, 0:8].unsqueeze(2).broadcast_to([P, HEADS, TOPK]), ALU.subtract)\
                        .then_inc(S["gate_d"], 1)
                    e.wait_ge(S["gate_e"], TT * layer + t + 1)
                    g = picks[:, t, 2, :].rearrange("p (h k) -> p h k", h=HEADS)
                    ch(v.tensor_reduce(small[:, 8:16], g, AX.X, ALU.add))
                    ch(v.reciprocal(small[:, 16:24], small[:, 8:16]))
                    tt(g, g, small[:, 16:24].unsqueeze(2).broadcast_to([P, HEADS, TOPK]), ALU.mult).then_inc(S["picks"], 1)
                for t in range(TT):
                    e.wait_ge(S["picks_turned"], TT * layer + t + 1)
                    for k in range(3):
                        v.tensor_copy(picksT[:, k, t * P:(t + 1) * P], PS[:, 6, k * P:(k + 1) * P]).then_inc(S["picksT"], 1)
                e.wait_ge(S["picksT"], 6 * (layer + 1))
                e.wait_ge(S["gelu_done"], layer + 1)

                def one_hot(i, b):
                    for j in range(4):
                        ins = ts(oh1[:, b, j, :], iota[:], picksT[:, 0, bass.ds(8 * i + 4 * b + j, 1)],
                                 picksT[:, 2, bass.ds(8 * i + 4 * b + j, 1)], ALU.is_equal, ALU.mult)
                    ins.then_inc(S["oh1_ready"], 1)

                with e.Fori(0, T // 8) as i:
                    for b in range(2):
                        n = layer * (T // 4) + b
                        e.wait_ge(S["g_ready_pad"], 2 * i + n + 1)
                        one_hot(i, b)
                    for b in range(2):
                        n = layer * (T // 4) + b
                        e.wait_ge(S["g_ready_pad"], 2 * i + n + 3)
                        c = C[:, :, bass.ds(8 * i + 4 * b, 4)]
                        tt(c, PS[:, 6 + b, :].rearrange("p (t k) -> p k t", t=4), c, ALU.mult).then_inc(S["g_taken_pad"], 1)
                e.wait_ge(S["tile_used"], SUMS[f"v{layer}"] + KEYS)
                for n in range(NC):
                    ins = residual(PS[:, 2 + n // 2, n % 2 * T:(n % 2 + 1) * T], layer, 5, n)
                ins.then_inc(S["x_new"], NC)
                e.wait_ge(S["x_new"], (2 * layer + 2) * NC)


def tiles(w):
    n = w.shape[1] // P
    return w.reshape(NC, P, n, P).transpose(2, 1, 0, 3).reshape(n, P, D)


def rows(a, chunks):
    return a.reshape(chunks, P).T


def constants():
    ident = np.eye(P, dtype=np.float32)
    axis = ROPE // 2
    half = axis // 2
    turn = np.zeros((ROPE, ROPE), np.float32)
    for a in range(2):
        for j in range(half):
            turn[a * axis + half + j, a * axis + j] = -1.0
            turn[a * axis + j, a * axis + half + j] = 1.0
    pos = np.arange(T)
    inv = (np.float32(10000.0) ** (-np.arange(0, axis, 2, dtype=np.float32) / np.float32(axis))).astype(np.float32)
    ang = np.stack([np.outer((pos // 64).astype(np.float32), inv), np.outer((pos % 64).astype(np.float32), inv)])
    ang = np.repeat(ang[:, None], 2, axis=1).transpose(0, 1, 3, 2).reshape(ROPE, T).astype(np.float32)
    cs = np.stack([np.cos(ang), np.sin(ang)], axis=1).astype(np.float32)
    cnt = np.stack([1.0 / (np.clip(pos + w - w // 2, 0, T) - np.clip(pos - w // 2, 0, T)) for w in WINDOWS])
    cnt = np.broadcast_to(cnt.astype(np.float32), (P, GROUPS, T))
    return ident, turn, cs, cnt


def kernel(**inputs):
    import concourse.bacc as bacc
    from concourse.bass_utils import run_bass_kernel_spmd

    a = {k: np.asarray(v) for k, v in inputs.items()}
    ident, turn, cs, cnt = constants()
    w_in = a["ab_w_in"][0]
    kv0, pool0 = Q_LORA + KV_LORA, Q_LORA + KV_LORA + ROPE
    cin = tiles(a["c_w_in"][0]).reshape(3, NC, P, D).transpose(1, 0, 2, 3).reshape(3 * NC, P, D)
    arrays = {
        "xT": a["x"][0].T.reshape(NC, P, T).transpose(1, 0, 2),
        "ctxT": a["ctx"][0].T.reshape(NC, P, T).transpose(1, 0, 2),
        "cT": np.stack([rows(a["c"][0], NC), rows(a["c_ctx"], NC)], axis=2),
        "mod_t": np.concatenate([tiles(a["mod_w"][i]) for i in range(LAYERS)]),
        "mod_b": rows(a["mod_b"], LAYERS * MODS * NC),
        "norms": np.stack([a["norm_mix"], a["norm_ffn"]]).reshape(2 * LAYERS * NC, P).T.reshape(P, 2, LAYERS, NC),
        "win_t": np.concatenate([tiles(w_in[:, :kv0]), tiles(w_in[:, pool0:])]),
        "wrope": w_in[:, kv0:pool0].reshape(NC, P, ROPE).transpose(1, 0, 2),
        "qa_g": rows(a["q_a_norm"][0], QC),
        "kva_g": rows(a["kv_a_norm"][0], KVC),
        "q_g": a["q_norm"][0][:, None],
        "k_g": a["k_norm"][0][:, None],
        "qb_w": a["q_b_w"][0].reshape(QC, P, -1).transpose(1, 0, 2),
        "kvb_w": a["kv_b_w"][0].reshape(KVC, P, -1).transpose(1, 0, 2),
        "pool_w": a["pool_w"][0].transpose(1, 0, 2),
        "pool_s": rows(a["pool_scale"][0], GROUPS),
        "wout_t": tiles(a["ab_w_out"][0]),
        "cin_t": cin,
        "conv_w": a["c_conv"][0].reshape(3, NC, P).transpose(2, 0, 1),
        "cout_t": tiles(a["c_w_out"][0]),
        "wq_t": np.stack([tiles(a["peer_wq"][i]) for i in range(LAYERS)]),
        "keys_t": a["peer_keys"].transpose(0, 2, 4, 1, 3).reshape(LAYERS, P, HEADS, KEYS),
        "u_t": a["peer_u"].reshape(LAYERS, KEYS, KEYS, NC, P).transpose(0, 1, 4, 3, 2).reshape(LAYERS, KEYS, P, D),
        "v_t": a["peer_v"].reshape(LAYERS, KEYS, P, D),
        "ident_c": ident, "rot_c": turn, "cs_c": cs, "cnt_c": cnt,
    }
    arrays = {k: np.ascontiguousarray(v) for k, v in arrays.items()}
    nc = bacc.Bacc("TRN2", target_bir_lowering=False, num_devices=1)
    args = {k: nc.dram_tensor(k, v.shape, F32, kind="ExternalInput").ap() for k, v in arrays.items()}
    args["out"] = nc.dram_tensor("out", (P, NC, T), F32, kind="ExternalOutput").ap()
    hybrid_kernel(nc, **args)
    got = run_bass_kernel_spmd(nc, [arrays], core_ids=[0]).results[0]["out"]
    return got.transpose(2, 1, 0).reshape(1, T, D)
```

```python
from contextlib import ExitStack

import numpy as np

import concourse.bass as bass
from concourse import mybir

F32 = mybir.dt.float32
F32R = mybir.dt.float32r
U32 = mybir.dt.uint32
ALU = mybir.AluOpType
ACT = mybir.ActivationFunctionType
AX = mybir.AxisListType

P = 128
D = 1024
NC = D // P
T = 256
TT = T // P
HEADS = 8
NOPE, ROPE, VH = 64, 32, 64
QH = NOPE + ROPE
Q_LORA, KV_LORA = 384, 256
QC, KVC = Q_LORA // P, KV_LORA // P
GROUPS = 4
WINDOWS = (2, 4, 8, 16)
PAD = 8
KEYS = 128
TOPK = 16
PICKS = HEADS * TOPK
EPS = 1e-6
LAYERS = 2
MODS = 6
ROWS = MODS * NC
SLOTS = 3
MSLOTS = 4
NEG = -3.0e38

STREAM = [("win", 9), ("wout", NC), ("wq0", HEADS), ("u0", KEYS), ("v0", KEYS),
          ("cin", 3 * NC), ("cout", NC), ("wq1", HEADS), ("u1", KEYS), ("v1", KEYS)]
TILE0, LINE0 = {}, {}
_n = _m = 0
for _name, _count in STREAM:
    TILE0[_name], LINE0[_name] = _n, _m
    _n += _count
    _m += _count if _name[0] != "v" else 0
COUNT = dict(STREAM)
TILES = _n
OUTS = [("ctx", KVC), ("rope", 2), ("qb", HEADS), ("kb", HEADS), ("vb", 4), ("poolw", GROUPS)]
OUT0, _n = {}, 0
for _name, _count in OUTS:
    OUT0[_name] = _n
    _n += _count
SECOND_SCORES, EXPS, SAFE, TURN, TURNED = 30, (30, 66), 96, 84, 90
TOPK_AT, PICKS_AT = (0, 38), (24, 62)
UNROLLED = 78


class Chain:

    def __init__(self, eng, sem):
        self.eng, self.sem, self.n, self.at = eng, sem, 0, None

    def value(self):
        return self.n if self.at is None else self.at + self.n

    def inc(self, ins):
        ins.then_inc(self.sem, 1)
        self.n += 1

    def wait(self):
        self.eng.wait_ge(self.sem, self.value())

    def __call__(self, ins):
        self.inc(ins)
        self.wait()

    def enter(self, i, per):
        self.start, self.per, self.at = self.n, per, i * per

    def leave(self, times):
        assert self.n - self.start == self.per
        self.n, self.at = self.start + times * self.per, None


def norms_at(k):
    return [(0, 0, 0), (0, 0, 1), (0, 3, 0), (1, 0, 0), (1, 3, 0)][k]


def hybrid_kernel(nc, xT, ctxT, c_rows, mod_t, mod_b, norms, win_t, wrope, qa_g, kva_g, q_g, k_g, qb_w, kvb_w, pool_w,
                  pool_s, wout_t, cin_t, conv_w, cout_t, wq_t, keys_t, u_t, v_t, ident_c, rot_c, cs_c, cnt_c, out):
    src = {"win": win_t, "wout": wout_t, "wq0": wq_t[0], "wq1": wq_t[1], "u0": u_t[0], "u1": u_t[1],
           "v0": v_t[0], "v1": v_t[1], "cin": cin_t, "cout": cout_t}
    with ExitStack() as ctx:
        def sb(name, shape, dt=F32):
            return ctx.enter_context(nc.sbuf_tensor(name, shape, dt))

        class Sems(dict):
            def __missing__(self, name):
                self[name] = ctx.enter_context(nc.semaphore(name))
                return self[name]

        S = Sems()
        PS = ctx.enter_context(nc.psum_tensor("PS", [P, 8, 512], F32))
        W = [sb(f"W{i}", [P, D]) for i in range(SLOTS)]
        WH = [sb(f"WH{i}", [P, D], F32R) for i in range(SLOTS)]
        WL = [sb(f"WL{i}", [P, D], F32R) for i in range(SLOTS)]
        x = sb("x", [P, NC, T])
        xh = sb("xh", [P, NC, T], F32R)
        xl = sb("xl", [P, NC, T], F32R)
        ch_ = sb("ch", [P, 2, T], F32R)
        cl_ = sb("cl", [P, 2, T], F32R)
        big = sb("big", [P, KEYS * T])
        C = big[:].rearrange("p (k t) -> p k t", t=T)
        oh1 = sb("oh1", [P, 4, 4, KEYS])
        oh2 = sb("oh2", [P, 4, 4, KEYS])
        M = [o[:, 2 * j:2 * j + 2].rearrange("p a b c -> p (a b c)") for o in (oh1, oh2) for j in range(2)]

        at = [0]

        def scratch(n, shape_str=None, dt=None, **kw):
            a = big[:, at[0]:at[0] + n]
            at[0] += n
            assert at[0] <= KEYS * T, at[0]
            if dt is not None:
                a = a.bitcast(dt)
            return a.rearrange(shape_str, **kw) if shape_str else a

        sq = scratch(4096)
        hp = scratch(GROUPS * (T + 2 * PAD), "p (g t) -> p g t", g=GROUPS)
        conv_at = at[0]
        ctx_x = scratch(NC * T, "p (c t) -> p c t", t=T)
        xmc = scratch(NC * T, "p (c t) -> p c t", t=T)
        att_at = at[0] - 2 * NC * T
        hq = scratch(QC * T, "p (c t) -> p c t", t=T)
        ckv = scratch(KVC * 2 * T, "p (c t) -> p c t", t=2 * T)
        kro = scratch(2 * T)
        ws = [scratch(T + 2 * PAD) for _ in range(2)]
        pooled = scratch(GROUPS * T, "p (g t) -> p g t", t=T)
        q_all = scratch(HEADS * T, "p (h t) -> p h t", t=T)
        k_all = scratch(HEADS * 2 * T, "p (h t) -> p h t", t=2 * T)
        v_at = at[0]
        v_all = scratch(4 * HEADS * VH, "p (k n) -> p k n", k=4)
        qbw = scratch(QC * HEADS * QH, "p (c n) -> p c n", c=QC)
        kvbw = scratch(KVC * HEADS * P, "p (c n) -> p c n", c=KVC)
        plw = scratch(GROUPS * P, "p (g n) -> p g n", g=GROUPS)
        cnt = scratch(GROUPS * T, "p (g t) -> p g t", g=GROUPS)
        wro = scratch(NC * ROPE, "p (c n) -> p c n", c=NC)
        cs = scratch(2 * T, "p (a t) -> p a t", a=2)
        mix = scratch(NC * T, "p (c t) -> p c t", t=T)
        rs = scratch(2048)
        xm = mix
        cbx = big[:, v_at:v_at + D]
        att = big[:, att_at:att_at + 3072]
        pe2 = att[:, 0:1024].rearrange("p (b n) -> p b n", b=2)
        pT = att[:, 1024:3072].rearrange("p (b k t) -> p b k t", b=2, k=4)
        at[0] = conv_at
        conv_u = scratch(2 * (T + 2), "p (b t) -> p b t", b=2)
        conv_s = scratch(T)
        conv_h = scratch(2 * 3 * T, "p (b k t) -> p b k t", b=2, k=3)
        at[0] = KEYS * T - 7680
        first_taken = at[0] // T
        picks = scratch(TT * 3 * PICKS, "p (t k n) -> p t k n", t=TT, k=3)
        sel_v = scratch(2 * TOPK, "p (a k) -> p a k", a=2)
        sel_f = scratch(2 * PICKS, "p (a h k) -> p a h k", a=2, h=HEADS)
        sel_i = scratch(2 * PICKS, "p (a h k) -> p a h k", U32, a=2, h=HEADS)
        rep = scratch(2 * KEYS)
        cand = scratch(TOPK * TOPK)
        top = scratch(PICKS, "p (h k) -> p h k", h=HEADS)
        pos = scratch(PICKS, dt=U32)
        dig = scratch(2 * PICKS, "p (a n) -> p a n", U32, a=2)
        eq = scratch(PICKS * TOPK, "p (n j) -> p n j", j=TOPK)
        keys = scratch(HEADS * KEYS, "p (h k) -> p h k", h=HEADS)
        q = scratch(HEADS * T, "p (h t) -> p h t", t=T)

        rinv = sb("rinv", [P, T])
        small = sb("small", [P, 64])
        eps = sb("eps", [P, 1])
        ones = sb("ones", [P, P])
        zero = sb("zero", [P, P])
        ident = sb("ident", [P, P])
        iota = sb("iota", [P, P])
        cb = sb("cb", [P, D])
        mod = sb("mod", [P, LAYERS * ROWS])
        modx = sb("modx", [P, 2 * NC])
        mods = sb("mods", [P, 12])
        modb = sb("modb", [P, LAYERS * ROWS])
        nrm = sb("nrm", [P, 2, LAYERS, NC])
        aff = sb("aff", [P, 5, NC])
        qag = sb("qag", [P, QC])
        kvag = sb("kvag", [P, KVC])
        qg = sb("qg", [P, 2])
        kg = sb("kg", [P, 1])
        pls = sb("pls", [P, GROUPS])
        cvw = sb("cvw", [P, 3, NC])
        rot = sb("rot", [P, ROPE])
        picksT = sb("picksT", [P, 3, T])
        second = sb("second", [P, 2, 4])
        y = big[:, 0:TT * D].rearrange("p (t d) -> p t d", t=TT)

        block = ctx.enter_context(nc.Block())

        @block.sync
        def _(e):
            def weights(name, j, i=None, per=6):
                n = TILE0[name] + j
                if i is None:
                    if n >= SLOTS:
                        e.wait_ge(S["low_ready"], n - SLOTS + 1)
                    s = src[name][j:j + 1]
                else:
                    e.wait_ge(S["low_ready"], per * i + n - SLOTS + 1)
                    s = src[name][bass.ds(per * i + j, 1)]
                e.dma_start(W[n % SLOTS][:], s.rearrange("a p n -> (a p) n")).then_inc(S[f"landed{n % SLOTS}"], 16)

            def rows_tile(m, i=None):
                if i is not None or m >= MSLOTS:
                    e.wait_ge(S["rows_used"], m - MSLOTS + 1 + (0 if i is None else 12 * i))
                s = mod_t[m:m + 1] if i is None else mod_t[bass.ds(12 * i + m, 1)]
                e.dma_start(M[m % MSLOTS], s.rearrange("a p n -> (a p) n")).then_inc(S[f"rows_landed{m % MSLOTS}"], 16)

            for dst, s in [(cb[:], c_rows[0:1, :].broadcast_to([P, D])), (cbx, c_rows[1:2, :].broadcast_to([P, D]))]:
                e.dma_start(dst, s).then_inc(S["cond"], 16)
            e.dma_start(x[:], xT).then_inc(S["x_landed"], 16)
            for m in range(4):
                rows_tile(m)
            e.dma_start(ctx_x, ctxT).then_inc(S["ctx_landed"], 16)
            for dst, s in [(modb[:], mod_b), (nrm[:], norms), (ident[:], ident_c)]:
                e.dma_start(dst, s).then_inc(S["base"], 16)
            for n in range(SLOTS):
                weights("win", n)
            for m in range(4, 2 * NC):
                rows_tile(m)
            for dst, s in [(wro, wrope), (qag[:], qa_g), (kvag[:], kva_g), (qg[0:QH, 0:1], q_g),
                           (kg[0:QH, :], k_g), (qbw, qb_w), (kvbw, kvb_w), (plw, pool_w), (pls[:], pool_s),
                           (cvw[:], conv_w), (rot[NOPE:QH, :], rot_c), (cs[NOPE:QH, :, :], cs_c), (cnt, cnt_c)]:
                e.dma_start(dst, s).then_inc(S["mixw"], 16)
            for m in range(2 * NC, 2 * NC + MSLOTS):
                rows_tile(m)
            m = 2 * NC + MSLOTS
            follow = {n: 1 for n in range(2 * SLOTS, 2 * SLOTS + COUNT["win"] - 1)}
            follow[14] = HEADS * TT + 1
            follow.update({15: 1, 16: 1, 17: 1})
            for n in range(SLOTS, TILE0["wq0"] + SLOTS):
                name = "win" if n < TILE0["wout"] else "wout" if n < TILE0["wq0"] else "wq0"
                if QC <= n - SLOTS < QC + KVC:
                    e.wait_ge(S["out_ready"], OUT0["ctx"] + n - SLOTS - QC + 1)
                weights(name, n - TILE0[name])
                for _ in range(follow.get(n, 0)):
                    rows_tile(m)
                    m += 1
            assert m == ROWS
            for layer in range(LAYERS):
                wq, u, v = f"wq{layer}", f"u{layer}", f"v{layer}"
                for j in range(SLOTS if layer == 0 else 0, HEADS):
                    weights(wq, j)
                e.wait_ge(S["x_split"], 3 * (layer + 1))
                e.dma_start(keys, keys_t[layer]).then_inc(S["keys_landed"], 16)
                with e.Fori(0, KEYS // 6) as i:
                    for j in range(6):
                        weights(u, j, i)
                for j in range(KEYS // 6 * 6, KEYS):
                    weights(u, j)
                done = 3
                for j in range(done):
                    weights(v, j)
                if layer == 0:
                    e.wait_ge(S["g_ready"], 4 + T // 4)
                    with e.Fori(0, 4) as i:
                        for j in range(24):
                            weights(v, done + j, i, 24)
                            if j % 2 == 1:
                                rows_tile(ROWS + j // 2, i)
                    done += 96
                turns = (KEYS - done) // 6
                with e.Fori(0, turns) as i:
                    for j in range(6):
                        weights(v, done + j, i)
                for j in range(done + 6 * turns, KEYS):
                    weights(v, j)
                if layer == 0:
                    with e.Fori(0, NC // 2) as i:
                        for j in range(6):
                            weights("cin", j, i)
                    for j in range(NC):
                        weights("cout", j)
            e.wait_ge(S["x_new"], 4 * NC)
            e.dma_start(out, x[:]).then_inc(S["stored"], 16)
            e.wait_ge(S["stored"], 16)

        @block.gpsimd
        def _(e):
            nc.gpsimd.memset(ones[:], 1.0).then_inc(S["const"], 1)
            nc.gpsimd.memset(zero[:], 0.0).then_inc(S["const"], 1)
            nc.gpsimd.memset(eps[:], EPS).then_inc(S["const"], 1)
            nc.gpsimd.iota(iota[:], [[1, P]], base=0, channel_multiplier=0,
                           allow_small_or_imprecise_dtypes=True).then_inc(S["const"], 1)
            e.wait_ge(S["const"], 4)
            ch = Chain(e, S["pool_chain"])
            for layer in range(LAYERS):
                e.wait_ge(S["picksT"], 6 * (layer + 1))
                with e.Fori(0, T // 16) as i:
                    ch.enter(i, 2)
                    for b in (1, 3):
                        e.wait_ge(S["g_ready"], 4 * i + layer * (T // 4) + b + 1)
                        ch.inc(nc.gpsimd.tensor_copy(second[:, b // 2, :], picksT[:, 1, bass.ds(16 * i + 4 * b, 4)]))
                        ch.wait()
                        e.sem_inc(S["pool_turn"], 1)
                        for j in range(4):
                            ins = nc.gpsimd.tensor_scalar(oh2[:, b, j, :], iota[:], second[:, b // 2, j:j + 1], None,
                                                          ALU.is_equal)
                        ins.then_inc(S["oh_pool"], 1)
                    ch.leave(T // 16)

        @block.tensor
        def _(e):
            mm = nc.tensor.matmul

            def linear(name, j, i=None, per=6):
                n, line, up = TILE0[name] + j, LINE0[name] + j, 0 if i is None else per * i
                e.wait_ge(S["low_ready"], up + n + 1)
                if line >= 2 or i is not None:
                    e.wait_ge(S["taken"], up + line - 1)
                o = PS[:, line % 2, 0:T]
                h, l = WH[n % SLOTS], WL[n % SLOTS]
                for c in range(NC):
                    mm(o, h[:, c * P:(c + 1) * P], xh[:, c, :], start=c == 0, stop=False)
                    mm(o, h[:, c * P:(c + 1) * P], xl[:, c, :], start=False, stop=False)
                    ins = mm(o, l[:, c * P:(c + 1) * P], xh[:, c, :], start=False, stop=c == NC - 1)
                ins.then_inc(S["used"], 1)

            def out_bank(name, j):
                n = OUT0[name] + j
                if n >= 2:
                    e.wait_ge(S["out_taken"], n - 1)
                return 4 + n % 2

            def norm(k, width=T, chunks=NC):
                e.wait_ge(S["norm_sq"], k + 1)
                for c in range(chunks):
                    ins = mm(PS[:, 7, 0:width], ones[:], sq[:, c * width:(c + 1) * width], start=c == 0, stop=c == chunks - 1)
                ins.then_inc(S["norm_ss"], 1)

            e.wait_ge(S["const"], 4)
            norm(0)
            norm(1)
            e.wait_ge(S["x_split"], 1)
            e.wait_ge(S["norm_out"], 2)
            e.wait_ge(S["mixw"], 13 * 16)
            for j in range(COUNT["win"]):
                if QC <= j < QC + KVC:
                    e.wait_ge(S[f"landed{j % SLOTS}"], 16 * (j // SLOTS + 1))
                    b = out_bank("ctx", j - QC)
                    for c in range(NC):
                        ins = mm(PS[:, b, 0:T], W[j % SLOTS][:, c * P:(c + 1) * P], xmc[:, c, :], start=c == 0, stop=c == NC - 1)
                    ins.then_inc(S["out_ready"], 1)
                linear("win", j)
            for o, r in enumerate((xmc, xm)):
                b = out_bank("rope", o)
                for c in range(NC):
                    ins = mm(PS[NOPE:QH, b, 0:T], wro[:, c, :], r[:, c, :], start=c == 0, stop=c == NC - 1)
                ins.then_inc(S["out_ready"], 1)
            norm(2, chunks=QC)
            for h in range(HEADS):
                if h == 0:
                    e.wait_ge(S["norm_out"], 3)
                b = out_bank("qb", h)
                for c in range(QC):
                    ins = mm(PS[0:QH, b, 0:T], qbw[:, c, h * QH:(h + 1) * QH], hq[:, c, :], start=c == 0, stop=c == QC - 1)
                ins.then_inc(S["out_ready"], 1)
            norm(3, width=2 * T, chunks=KVC)
            for h in range(HEADS):
                if h == 0:
                    e.wait_ge(S["norm_out"], 4)
                b = out_bank("kb", h)
                for c in range(KVC):
                    ins = mm(PS[0:NOPE, b, :], kvbw[:, c, h * P:h * P + NOPE], ckv[:, c, :], start=c == 0, stop=c == KVC - 1)
                ins.then_inc(S["out_ready"], 1)
            for kc in range(4):
                b = out_bank("vb", kc)
                for c in range(KVC):
                    ins = mm(PS[:, b, :], ckv[:, c, kc * P:(kc + 1) * P],
                             kvbw[:, c, :].rearrange("p (h n) -> p h n", h=HEADS)[:, :, NOPE:], start=c == 0,
                             stop=c == KVC - 1)
                ins.then_inc(S["out_ready"], 1)
            e.wait_ge(S["pooled"], GROUPS)
            for g in range(GROUPS):
                b = out_bank("poolw", g)
                mm(PS[:, b, 0:T], plw[:, g, :], pooled[:, g, :], start=True, stop=True).then_inc(S["out_ready"], 1)
            e.wait_ge(S["out_taken"], OUT0["poolw"] + GROUPS)
            for n in range(3):
                e.wait_ge(S["head_sq"], n + 1)
                if n:
                    e.wait_ge(S["head_rt"], n)
                for j in range(4):
                    ins = mm(PS[0:QH, 2 + j, :], ones[0:QH, 0:QH], sq[0:QH, j * 512:(j + 1) * 512], start=True, stop=True)
                ins.then_inc(S["head_ss"], 1)
            for n, a in enumerate([q_all, k_all]):
                e.wait_ge(S["head_n"], n + 1)
                e.wait_ge(S["head_rt"], 3)
                if n == 1:
                    e.wait_ge(S["roped"], 1)
                for j in range(4):
                    r = a[NOPE:QH, 2 * j:2 * j + 2, :] if n == 0 else a[NOPE:QH, 2 * j:2 * j + 2, T:]
                    ins = mm(PS[NOPE:QH, 2 + j, :], rot[NOPE:QH, :], r, start=True, stop=True)
                ins.then_inc(S["rot"], 1)
            e.wait_ge(S["roped"], 2)

            def scores(k):
                h, t = divmod(k, TT)
                if k >= 2:
                    e.wait_ge(S["att_exp"], k - 1)
                mm(PS[:, 2 + k % 2, :], q_all[0:QH, h, t * P:(t + 1) * P], k_all[0:QH, h, :], start=True,
                   stop=True).then_inc(S["att_s"], 1)

            def turn(k):
                e.wait_ge(S["att_p"], k + 1)
                if k >= 2:
                    e.wait_ge(S["att_c"], k - 1)
                for j in range(4):
                    ins = nc.tensor.transpose(PS[:, 4 + k % 2, j * P:(j + 1) * P], pe2[:, k % 2, j * P:(j + 1) * P], ident[:])
                ins.then_inc(S["att_t"], 1)

            def values(h):
                e.wait_ge(S["att_c"], 2 * h + 2)
                if h >= 2:
                    e.wait_ge(S["att_o"], h - 1)
                lo = h % 2 * VH
                for j in range(4):
                    ins = mm(PS[lo:lo + VH, 6 + h % 2, 0:T], v_all[:, j, h * VH:(h + 1) * VH], pT[:, h % 2, j, :],
                             start=j == 0, stop=j == 3)
                ins.then_inc(S["att_v"], 1)

            scores(0)
            scores(1)
            for k in range(HEADS * TT):
                turn(k)
                if k + 2 < HEADS * TT:
                    scores(k + 2)
                if k % 2 == 1:
                    values(k // 2)
            e.wait_ge(S["x_split"], 2)
            for n in range(NC):
                linear("wout", n)

            for layer in range(LAYERS):
                if layer == 1:
                    norm(5)
                    e.wait_ge(S["x_split"], 4)
                    with e.Fori(0, NC // 2) as i:
                        for j in range(6):
                            linear("cin", j, i)
                    e.wait_ge(S["x_split"], 5)
                    for n in range(NC):
                        linear("cout", n)
                norm(4 if layer == 0 else 6)
                e.wait_ge(S["x_split"], 3 * (layer + 1))
                for h in range(HEADS):
                    linear(f"wq{layer}", h)
                u, v = f"u{layer}", f"v{layer}"

                def key_scores(t):
                    if t:
                        e.wait_ge(S["topk_read"], HEADS * (TT * layer + t))
                    for half in range(2):
                        lo = half * 64
                        for h in range(HEADS):
                            ins = mm(PS[:, 2 + 2 * half + h // 4, h % 4 * P:(h % 4 + 1) * P],
                                     q[lo:lo + 64, h, t * P:(t + 1) * P], keys[lo:lo + 64, h, :], start=True, stop=True)
                    ins.then_inc(S["scores_ready"], 1)

                def blocks(first, last):
                    with e.Fori(0, (last - first) // 6) as i:
                        for j in range(6):
                            linear(u, first + j, i)

                e.wait_ge(S["keys_landed"], 16 * (layer + 1))
                e.wait_ge(S["taken"], LINE0[u])
                key_scores(0)
                blocks(0, SECOND_SCORES)
                key_scores(1)
                blocks(SECOND_SCORES, TURN)
                for t in range(TT):
                    e.wait_ge(S["picks"], TT * layer + t + 1)
                    for k in range(3):
                        ins = nc.tensor.transpose(PS[:, 6 + t, k * P:(k + 1) * P], picks[:, t, k, :], ident[:])
                    ins.then_inc(S["picks_turned"], 1)
                blocks(TURN, 126)
                linear(u, 126)
                linear(u, 127)
                e.wait_ge(S["topk_read"], HEADS * TT * (layer + 1))
                with e.Fori(0, T // 16) as i:
                    for b in range(4):
                        n = layer * (T // 4)
                        e.wait_ge(S["g_taken"], 4 * i + n + b + 1)
                        if b % 2 == 0:
                            e.wait_ge(S["oh_dve"], 2 * i + n // 2 + b // 2 + 1)
                        else:
                            e.wait_ge(S["oh_act"], 2 * i + n // 2 + b // 2 + 1)
                            e.wait_ge(S["oh_pool"], 2 * i + n // 2 + b // 2 + 1)
                        for j in range(4):
                            ins = mm(PS[:, 2 + b, j * P:(j + 1) * P], oh2[:, b, j, :], oh1[:, b, j, :], start=True, stop=True)
                        ins.then_inc(S["g_ready"], 1)
                e.wait_ge(S["g_taken"], 4 + (layer + 1) * (T // 4))
                for b in range(4):
                    mm(PS[:, 2 + b, :], zero[:], x[:, 0:2, :], start=True, stop=False, skip_group_check=True)

                def second_product(j, i=None):
                    n, up = TILE0[v] + j, 0 if i is None else 6 * i
                    e.wait_ge(S["low_ready"], up + n + 1)
                    e.wait_ge(S["c_low"], up + layer * KEYS + j + 1)
                    h, l = WH[n % SLOTS], WL[n % SLOTS]
                    for t in range(TT):
                        for c, w in ((ch_, h), (ch_, l), (cl_, h)):
                            for k in range(2):
                                ins = mm(PS[:, 2 + 2 * t + k, :], c[:, j % 2, t * P:(t + 1) * P], w[:, k * 512:(k + 1) * 512],
                                         start=False, stop=False, skip_group_check=True)
                    ins.then_inc(S["used"], 1)

                with e.Fori(0, 20) as i:
                    for j in range(6):
                        second_product(j, i)
                for j in range(120, KEYS):
                    second_product(j)
                for t in range(TT):
                    e.wait_ge(S[f"y_out{t}"], layer + 1)
                    for c in range(NC):
                        b = (0, 1, 6, 7)[c // 2]
                        ins = nc.tensor.transpose(PS[:, b, c % 2 * T + t * P:c % 2 * T + (t + 1) * P],
                                                  y[:, t, c * P:(c + 1) * P], ident[:])
                ins.then_inc(S["y_turned"], 1)

        @block.scalar
        def _(e):
            act = nc.scalar.activation
            ch = Chain(e, S["act_chain"])

            def high(n, up=0):
                if n >= SLOTS:
                    e.wait_ge(S["used"], up + n - SLOTS + 1)
                e.wait_ge(S[f"landed{n % SLOTS}"], 16 * (n // SLOTS + 1) + (0 if isinstance(up, int) else up_slots[0]))
                act(WH[n % SLOTS][:], W[n % SLOTS][:], ACT.Copy).then_inc(S["high_ready"], 1)

            up_slots = [0]

            def line(name, j, up=0):
                e.wait_ge(S["used"], up + TILE0[name] + j + 1)
                return PS[:, (LINE0[name] + j) % 2, 0:T]

            def ready(name, j):
                n = OUT0[name] + j
                e.wait_ge(S["out_ready"], n + 1)
                return PS[:, 4 + n % 2, :]

            def squares(a, n):
                act(sq[:, 0:n], a, ACT.Square).then_inc(S["norm_sq"], 1)

            def root(k, n, width=T):
                e.wait_ge(S["norm_ss"], k + 1)
                if k:
                    e.wait_ge(S["norm_out"], k)
                r = rinv[:] if width == T else rs[:, 0:width]
                act(r, PS[:, 7, 0:width], ACT.Sqrt, bias=eps[:], scale=width / (n * P)).then_inc(S["norm_rt"], 1)

            e.wait_ge(S["cond"], 32)
            act(cb[:], cb[:], ACT.Silu).then_inc(S["silu"], 1)
            act(cbx, cbx, ACT.Silu).then_inc(S["silu"], 1)
            e.wait_ge(S["const"], 4)
            e.wait_ge(S["x_landed"], 16)
            squares(x[:], NC * T)
            root(0, NC * T)
            e.wait_ge(S["ctx_landed"], 16)
            squares(ctx_x, NC * T)
            for n in range(SLOTS):
                high(n)
            root(1, NC * T)
            for j in range(COUNT["win"]):
                if QC <= j < QC + KVC:
                    act(ckv[:, j - QC, 0:T], ready("ctx", j - QC)[:, 0:T], ACT.Copy).then_inc(S["out_taken"], 1)
                high(j + SLOTS)
                if j < QC:
                    dst = hq[:, j, :]
                elif j < QC + KVC:
                    dst = ckv[:, j - QC, T:2 * T]
                else:
                    e.wait_ge(S["pad_zero"], 1)
                    dst = hp[:, j - QC - KVC, PAD:PAD + T]
                act(dst, line("win", j), ACT.Copy).then_inc(S["taken"], 1)
            for side in range(2):
                act(kro[NOPE:QH, side * T:(side + 1) * T], ready("rope", side)[NOPE:QH, 0:T], ACT.Copy)\
                    .then_inc(S["out_taken"], 1)
            e.wait_ge(S["taken"], COUNT["win"])
            squares(hq, QC * T)
            root(2, QC * T)
            for h in range(HEADS):
                act(q_all[0:QH, h, :], ready("qb", h)[0:QH, 0:T], ACT.Copy).then_inc(S["out_taken"], 1)
            squares(ckv, KVC * 2 * T)
            root(3, KVC * 2 * T, width=2 * T)
            for h in range(HEADS):
                act(k_all[0:NOPE, h, :], ready("kb", h)[0:NOPE, :], ACT.Copy).then_inc(S["out_taken"], 1)
            for kc in range(4):
                act(v_all[:, kc, :], ready("vb", kc), ACT.Copy).then_inc(S["out_taken"], 1)
            for g in range(GROUPS):
                act(mix[:, 4 + g, :], ready("poolw", g)[:, 0:T], ACT.Copy, scale=pls[:, g:g + 1])\
                    .then_inc(S["out_taken"], 1)
            e.wait_ge(S["k_rope"], 1)
            e.wait_ge(S["out_taken"], OUT0["poolw"])
            e.wait_ge(S["norm_out"], 4)
            for n in range(3):
                a = q_all[0:QH] if n == 0 else k_all[0:QH, 4 * (n - 1):4 * n, :]
                act(sq[0:QH, 0:2048], a, ACT.Square).then_inc(S["head_sq"], 1)
                e.wait_ge(S["head_ss"], n + 1)
                if n:
                    e.wait_ge(S["head_rs"], n)
                act(rs[0:QH, :], PS[0:QH, 2:6, :], ACT.Sqrt, bias=eps[0:QH, :], scale=1.0 / QH).then_inc(S["head_rt"], 1)

            def exps(k):
                e.wait_ge(S["att_m"], k + 1)
                if k >= 2:
                    e.wait_ge(S["att_t"], k - 1)
                act(pe2[:, k % 2, :], PS[:, 2 + k % 2, :], ACT.Exp, bias=small[:, k:k + 1],
                    accum_out=small[:, 16 + k:17 + k]).then_inc(S["att_exp"], 1)

            exps(0)
            for k in range(HEADS * TT):
                if k + 1 < HEADS * TT:
                    exps(k + 1)
                h, t = divmod(k, TT)
                e.wait_ge(S["att_t"], k + 1)
                if h >= 2:
                    e.wait_ge(S["att_v"], h - 1)
                act(pT[:, h % 2, :, t * P:(t + 1) * P],
                    PS[:, 4 + k % 2, :].rearrange("p (j t) -> p j t", j=4), ACT.Copy).then_inc(S["att_c"], 1)
            for n in range(NC):
                high(TILE0["wout"] + n + SLOTS)

            for layer in range(LAYERS):
                u, v = f"u{layer}", f"v{layer}"
                if layer == 1:
                    e.wait_ge(S["x_new"], 2 * NC)
                    squares(x[:], NC * T)
                    root(5, NC * T)
                    with e.Fori(0, NC // 2) as i:
                        up_slots[0] = 32 * i
                        for j in range(6):
                            high(TILE0["cin"] + j + SLOTS, 6 * i)
                            n, k = divmod(j, 3)
                            if k == 0:
                                e.wait_ge(S["conv_taken"], 2 * i + n + 1)
                            act(conv_h[:, n, k, :], line("cin", j, 6 * i), ACT.Copy).then_inc(S["taken"], 1)
                    for n in range(NC):
                        high(TILE0["cout"] + n + SLOTS)
                e.wait_ge(S["x_new"], (2 * layer + 1) * NC)
                squares(x[:], NC * T)
                root(4 if layer == 0 else 6, NC * T)
                for h in range(HEADS):
                    high(TILE0[f"wq{layer}"] + h + SLOTS)
                    act(q[:, h, :], line(f"wq{layer}", h), ACT.Copy).then_inc(S["taken"], 1)

                def blocks(first, last):
                    with e.Fori(0, (last - first) // 6) as i:
                        up_slots[0] = 32 * i
                        for j in range(6):
                            high(TILE0[u] + first + j + SLOTS, 6 * i)
                            act(C[:, bass.ds(6 * i + first + j, 1), :], line(u, first + j, 6 * i), ACT.Gelu)\
                                .then_inc(S["taken"], 1)

                def gate_exp(t):
                    e.wait_ge(S["gate_d"], TT * layer + t + 1)
                    act(picks[:, t, 2, :], top, ACT.Exp).then_inc(S["gate_e"], 1)

                blocks(0, EXPS[0])
                gate_exp(0)
                blocks(EXPS[0], EXPS[1])
                gate_exp(1)
                blocks(EXPS[1], SAFE)
                e.wait_ge(S["picks_turned"], TT * (layer + 1))
                blocks(SAFE, 126)
                for j in (126, 127):
                    high(TILE0[u] + j + SLOTS)
                    act(C[:, j, :], line(u, j), ACT.Gelu).then_inc(S["taken"], 1)
                e.wait_ge(S["picksT"], 6 * (layer + 1))
                with e.Fori(0, T // 16) as i:
                    ch.enter(i, 2)
                    for b in (1, 3):
                        e.wait_ge(S["g_ready"], 4 * i + layer * (T // 4) + b + 1)
                        for j in range(4):
                            ins = act(oh1[:, b, j, :], iota[:], ACT.Abs, scale=-1.0,
                                      bias=picksT[:, 0, bass.ds(16 * i + 4 * b + j, 1)])
                        ch(ins)
                        for j in range(4):
                            ins = act(oh1[:, b, j, :], oh1[:, b, j, :], ACT.Relu, scale=-1.0,
                                      bias=picksT[:, 2, bass.ds(16 * i + 4 * b + j, 1)])
                        ins.then_inc(S["oh_act"], 1)
                    ch.leave(T // 16)

                def c_high(j, up=0):
                    if j >= 2:
                        e.wait_ge(S["used"], up + TILE0[v] + j - 1)
                    src_ = C[:, j, :] if isinstance(up, int) else C[:, bass.ds(up + j, 1), :]
                    act(ch_[:, j % 2, :], src_, ACT.Copy).then_inc(S["c_high"], 1)

                e.wait_ge(S["g_taken"], 4 + (layer + 1) * (T // 4))
                c_high(0)
                c_high(1)
                with e.Fori(0, 20) as i:
                    up_slots[0] = 32 * i
                    for j in range(6):
                        c_high(j + 2, 6 * i)
                        high(TILE0[v] + j + SLOTS, 6 * i)
                for j in range(120, KEYS):
                    if j + 2 < KEYS:
                        c_high(j + 2)
                    if TILE0[v] + j + SLOTS < TILES:
                        high(TILE0[v] + j + SLOTS)
                e.wait_ge(S["used"], TILE0[v] + KEYS)
                e.wait_ge(S["c_low"], (layer + 1) * KEYS)
                act(y[:, 0, :], PS[:, 2:4, :], ACT.Copy).then_inc(S["y_out0"], 1)

        @block.vector
        def _(e):
            v_ = nc.vector
            ch = Chain(e, S["dve_chain"])
            tt, stt, ts = v_.tensor_tensor, v_.scalar_tensor_tensor, v_.tensor_scalar

            def low(n, up=0):
                e.wait_ge(S["high_ready"], up + n + 1)
                tt(WL[n % SLOTS][:], W[n % SLOTS][:], WH[n % SLOTS][:].bitcast(F32), ALU.subtract).then_inc(S["low_ready"], 1)

            def row(m, dst=None, i=None):
                e.wait_ge(S[f"rows_landed{m % MSLOTS}"], 16 * (m // MSLOTS + 1) + (0 if i is None else i))
                w = M[m % MSLOTS]
                v_.tensor_tensor_reduce(out=w, in0=w, in1=cb[:], scale=1.0, scalar=0.0, op0=ALU.mult, op1=ALU.add,
                                        accum_out=mod[:, m:m + 1] if dst is None else dst).then_inc(S["rows_used"], 1)

            def add_bias(first, last):
                e.wait_ge(S["rows_used"], last)
                ch(tt(mod[:, first:last], mod[:, first:last], modb[:, first:last], ALU.add))

            def line(name, j):
                e.wait_ge(S["used"], TILE0[name] + j + 1)
                return PS[:, (LINE0[name] + j) % 2, 0:T]

            def mrow(layer, k, col=0):
                a = layer * ROWS + k * NC
                return modx[:, k * NC:(k + 1) * NC] if col else mod[:, a:a + NC]

            def gains(k):
                layer, r, col = norms_at(k)
                ch(stt(aff[:, k, :], mrow(layer, r + 1, col), 1.0, nrm[:, 0 if r == 0 else 1, layer, :], ALU.add, ALU.mult))

            def norm(k, src_, dst, which=None, gain=None, chunks=NC, width=T):
                e.wait_ge(S["norm_rt"], k + 1)
                r = rinv[:] if width == T else rs[:, 0:width]
                ch(v_.reciprocal(r, r))
                for c in range(chunks):
                    g = gain[:, c:c + 1] if which is None else aff[:, which, c:c + 1]
                    ch.inc(stt(dst[:, c, :], src_[:, c, :], g, r, ALU.mult, ALU.mult))
                ch.wait()
                if which is not None:
                    layer, r_, col = norms_at(which)
                    for c in range(chunks):
                        ch.inc(ts(dst[:, c, :], dst[:, c, :], mrow(layer, r_, col)[:, c:c + 1], None, ALU.add))
                    ch.wait()
                e.nop().then_inc(S["norm_out"], 1)

            def split(a, first=0, last=NC, done=True):
                ch(v_.tensor_copy(xh[:, first:last, :], a[:, first:last, :]))
                ins = tt(xl[:, first:last, :], a[:, first:last, :], xh[:, first:last, :].bitcast(F32), ALU.subtract)
                if done:
                    ins.then_inc(S["x_split"], 1)

            def residual(a, layer, r, n):
                return stt(x[:, n, :], a, mrow(layer, r)[:, n:n + 1], x[:, n, :], ALU.mult, ALU.add)

            v_.memset(small[:, 63:64], 0.0).then_inc(S["g_ready"], 4)
            v_.memset(small[:, 62:63], 0.0).then_inc(S["g_taken"], 4)
            v_.memset(small[:, 61:62], 0.0).then_inc(S["conv_taken"], 2)
            v_.memset(hp, 0.0).then_inc(S["pad_zero"], 1)
            e.wait_ge(S["silu"], 2)
            for m in range(2 * NC):
                e.wait_ge(S[f"rows_landed{m % MSLOTS}"], 16 * (m // MSLOTS + 1))
                ch(v_.tensor_tensor_reduce(out=rs[:, 0:D], in0=M[m % MSLOTS], in1=cbx, scale=1.0, scalar=0.0, op0=ALU.mult,
                                           op1=ALU.add, accum_out=modx[:, m:m + 1]))
                row(m)
            e.wait_ge(S["base"], 3 * 16)
            add_bias(0, 2 * NC)
            ch(tt(modx[:], modx[:], modb[:, 0:2 * NC], ALU.add))
            gains(0)
            gains(1)
            norm(0, x, xm, which=0)
            split(xm)
            for n in range(SLOTS):
                low(n)
            norm(1, ctx_x, xmc, which=1)
            for n in range(COUNT["win"]):
                low(n + SLOTS)
                row(2 * NC + n)
            add_bias(2 * NC, 3 * NC)
            e.wait_ge(S["mixw"], 13 * 16)
            ch(ts(qg[0:QH, 1:2], qg[0:QH, 0:1], float(QH) ** -0.5, None, ALU.mult))
            norm(2, hq, hq, gain=qag, chunks=QC)
            e.wait_ge(S["taken"], COUNT["win"])
            for g, w in enumerate(WINDOWS):
                cur, n, size = hp[:, g, :], T + 2 * PAD, 1
                k = 0
                while size < w:
                    n -= size
                    ch(tt(ws[k % 2][:, 0:n], cur[:, 0:n], cur[:, size:size + n], ALU.add))
                    cur = ws[k % 2]
                    k += 1
                    size *= 2
                a = PAD - w // 2
                ch(tt(pooled[:, g, :], cur[:, a:a + T], cnt[:, g, :], ALU.mult))
                ch(tt(pooled[:, g, :], pooled[:, g, :], hp[:, g, PAD:PAD + T], ALU.subtract))
            e.nop().then_inc(S["pooled"], GROUPS)
            norm(3, ckv, ckv, gain=kvag, chunks=KVC, width=2 * T)
            e.wait_ge(S["out_taken"], OUT0["qb"])
            v_.tensor_copy(k_all[NOPE:QH], kro[NOPE:QH, :].unsqueeze(1).broadcast_to([ROPE, HEADS, 2 * T]))\
                .then_inc(S["k_rope"], 1)
            for n in range(3):
                e.wait_ge(S["head_rt"], n + 1)
                ch(v_.reciprocal(rs[0:QH, :], rs[0:QH, :]))
                a = q_all[0:QH] if n == 0 else k_all[0:QH, 4 * (n - 1):4 * n, :]
                a = a.rearrange("p h t -> p (h t)")
                g = qg[0:QH, 1:2] if n == 0 else kg[0:QH, :]
                ch(stt(a, a, g, rs[0:QH, :], ALU.mult, ALU.mult))
                e.nop().then_inc(S["head_rs"], 1)
                if n != 1:
                    e.nop().then_inc(S["head_n"], 1)
            for n, a in enumerate([q_all[NOPE:QH], k_all[NOPE:QH, :, T:]]):
                e.wait_ge(S["rot"], n + 1)
                t2 = rs[NOPE:QH, :].rearrange("p (h t) -> p h t", t=T)
                sin = cs[NOPE:QH, 1, :].unsqueeze(1).broadcast_to([ROPE, HEADS, T])
                cos = cs[NOPE:QH, 0, :].unsqueeze(1).broadcast_to([ROPE, HEADS, T])
                ch(tt(t2, PS[NOPE:QH, 2:6, :].rearrange("p b (h t) -> p (b h) t", t=T), sin, ALU.mult))
                ch(tt(a, a, cos, ALU.mult))
                tt(a, a, t2, ALU.add).then_inc(S["roped"], 1)
                e.wait_ge(S["roped"], n + 1)

            def maxes(k):
                e.wait_ge(S["att_s"], k + 1)
                v_.tensor_reduce(small[:, k:k + 1], PS[:, 2 + k % 2, :], AX.X, ALU.max, negate=True).then_inc(S["att_m"], 1)

            maxes(0)
            for k in range(HEADS * TT):
                if k + 1 < HEADS * TT:
                    maxes(k + 1)
                e.wait_ge(S["att_exp"], k + 1)
                ch(v_.reciprocal(small[:, 32 + k % 8:33 + k % 8], small[:, 16 + k:17 + k]))
                ts(pe2[:, k % 2, :], pe2[:, k % 2, :], small[:, 32 + k % 8:33 + k % 8], None, ALU.mult).then_inc(S["att_p"], 1)
                if k % 2 == 1 and k >= 3:
                    done = k // 2 - 1
                    e.wait_ge(S["att_v"], done + 1)
                    lo = done % 2 * VH
                    v_.tensor_copy(mix[lo:lo + VH, done // 2, :], PS[lo:lo + VH, 6 + done % 2, 0:T])\
                        .then_inc(S["att_o"], 1)
                row(3 * NC + 1 + k)
            e.wait_ge(S["out_taken"], OUT0["poolw"] + GROUPS)
            split(mix, 4, 8, done=False)
            e.wait_ge(S["att_v"], HEADS)
            v_.tensor_copy(mix[VH:, HEADS // 2 - 1, :], PS[VH:, 7, 0:T]).then_inc(S["att_o"], 1)
            e.wait_ge(S["att_o"], HEADS)
            split(mix, 0, 4)
            for n in range(NC):
                low(TILE0["wout"] + n + SLOTS)
                residual(line("wout", n), 0, 2, n).then_inc(S["taken"], 1)
                if n < NC - 1:
                    row(ROWS - NC + 1 + n)
            e.wait_ge(S["taken"], LINE0["wout"] + NC)
            e.nop().then_inc(S["x_new"], NC)
            add_bias(3 * NC, ROWS)
            gains(2)

            for layer in range(LAYERS):
                u, v = f"u{layer}", f"v{layer}"
                if layer == 1:
                    norm(5, x, xm, which=3)
                    split(xm)
                    ch(v_.memset(conv_u, 0.0))
                    with e.Fori(0, NC // 2) as i:
                        ch.enter(i, 8)
                        for n in range(2):
                            for k in range(3):
                                low(TILE0["cin"] + 3 * n + k + SLOTS, 6 * i)
                            e.wait_ge(S["taken"], 6 * i + LINE0["cin"] + 3 * n + 3)
                            h_ = conv_h[:, n]
                            u_ = conv_u[:, n]
                            ch(tt(u_[:, 1:T + 1], h_[:, 1, :], h_[:, 2, :], ALU.mult))
                            ch(ts(conv_s, u_[:, 0:T], cvw[:, 0, bass.ds(2 * i + n, 1)], None, ALU.mult))
                            ch(stt(conv_s, u_[:, 1:T + 1], cvw[:, 1, bass.ds(2 * i + n, 1)], conv_s, ALU.mult, ALU.add))
                            ch(stt(conv_s, u_[:, 2:T + 2], cvw[:, 2, bass.ds(2 * i + n, 1)], conv_s, ALU.mult, ALU.add))
                            tt(mix[:, bass.ds(2 * i + n, 1), :], h_[:, 0, :], conv_s, ALU.mult).then_inc(S["conv_taken"], 1)
                            e.wait_ge(S["conv_taken"], 2 * i + n + 3)
                        ch.leave(NC // 2)
                    e.wait_ge(S["used"], TILE0["cout"])
                    split(mix)
                    for n in range(NC):
                        low(TILE0["cout"] + n + SLOTS)
                        residual(line("cout", n), 1, 2, n).then_inc(S["taken"], 1)
                    e.wait_ge(S["taken"], LINE0["cout"] + NC)
                    e.nop().then_inc(S["x_new"], NC)
                norm(4 if layer == 0 else 6, x, xm, which=2 if layer == 0 else 4)
                split(xm)
                for h in range(HEADS):
                    low(TILE0[f"wq{layer}"] + h + SLOTS)

                def key_topk(t, h, half):
                    if h == 0 and half == 0:
                        e.wait_ge(S["scores_ready"], TT * layer + t + 1)
                    s = PS[:, 2 + 2 * half + h // 4, h % 4 * P:(h % 4 + 1) * P]
                    lo, hi = sel_v[:, half, 0:8], sel_v[:, half, 8:16]
                    ch(v_.max(lo, s))
                    ch.inc(v_.max_index(sel_i[:, half, h, 0:8], lo, s))
                    ch(v_.match_replace(rep[:, 0:KEYS], lo, s, NEG))
                    ch(v_.max(hi, rep[:, 0:KEYS]))
                    ch(v_.max_index(sel_i[:, half, h, 8:16], hi, rep[:, 0:KEYS]))

                def pair_topk(h):
                    e.nop().then_inc(S["topk_read"], 1)
                    ch(tt(cand.rearrange("p (a b) -> p a b", a=TOPK), sel_v[:, 0, :].unsqueeze(2).broadcast_to([P, TOPK, TOPK]),
                          sel_v[:, 1, :].unsqueeze(1).broadcast_to([P, TOPK, TOPK]), ALU.add))
                    ps = pos[:, h * TOPK:(h + 1) * TOPK]
                    ch(v_.max(top[:, h, 0:8], cand))
                    ch.inc(v_.max_index(ps[:, 0:8], top[:, h, 0:8], cand))
                    ch(v_.match_replace(rep, top[:, h, 0:8], cand, NEG))
                    ch(v_.max(top[:, h, 8:16], rep))
                    ch(v_.max_index(ps[:, 8:16], top[:, h, 8:16], rep))

                def find(t, part):
                    e4 = eq.rearrange("p (h k) j -> p h k j", h=HEADS)
                    half = 0 if part < 6 else 1
                    if part == 0:
                        ch(v_.tensor_copy(small[:, 0:8], top[:, :, 0]))
                        tt(top, top, small[:, 0:8].unsqueeze(2).broadcast_to([P, HEADS, TOPK]), ALU.subtract)\
                            .then_inc(S["gate_d"], 1)
                        ch(v_.tensor_copy(sel_f, sel_i))
                        ch(ts(dig[:, 0, :], pos, 4, None, ALU.logical_shift_right))
                        ch(ts(dig[:, 1, :], pos, 15, None, ALU.bitwise_and))
                    elif part in (1, 6):
                        ch(tt(eq, dig[:, half, :].unsqueeze(2).broadcast_to([P, PICKS, TOPK]),
                              iota[:, 0:TOPK].unsqueeze(1).broadcast_to([P, PICKS, TOPK]), ALU.is_equal))
                    elif part in (3, 8):
                        ch(tt(e4, e4, sel_f[:, half].unsqueeze(2).broadcast_to([P, HEADS, TOPK, TOPK]), ALU.mult))
                    elif part in (4, 10):
                        ch(v_.tensor_reduce(picks[:, t, half, :], eq, AX.X, ALU.add))
                    elif part == 12:
                        e.wait_ge(S["gate_e"], TT * layer + t + 1)
                        g = picks[:, t, 2, :].rearrange("p (h k) -> p h k", h=HEADS)
                        ch(v_.tensor_reduce(small[:, 8:16], g, AX.X, ALU.add))
                        ch(v_.reciprocal(small[:, 16:24], small[:, 8:16]))
                        tt(g, g, small[:, 16:24].unsqueeze(2).broadcast_to([P, HEADS, TOPK]), ALU.mult)\
                            .then_inc(S["picks"], 1)

                for j in range(UNROLLED):
                    low(TILE0[u] + j + SLOTS)
                    for t in range(TT):
                        h, part = divmod(j - TOPK_AT[t], 3)
                        if 0 <= h < HEADS:
                            if part < 2:
                                key_topk(t, h, part)
                            else:
                                pair_topk(h)
                        if 0 <= j - PICKS_AT[t] <= 12:
                            find(t, j - PICKS_AT[t])

                def lows(first, last):
                    with e.Fori(0, (last - first) // 6) as i:
                        for j in range(6):
                            low(TILE0[u] + first + j + SLOTS, 6 * i)

                lows(UNROLLED, TURNED)
                for t in range(TT):
                    e.wait_ge(S["picks_turned"], TT * layer + t + 1)
                    for k in range(3):
                        v_.tensor_copy(picksT[:, k, t * P:(t + 1) * P], PS[:, 6 + t, k * P:(k + 1) * P])\
                            .then_inc(S["picksT"], 1)
                lows(TURNED, 126)
                for j in (126, 127):
                    low(TILE0[u] + j + SLOTS)
                e.wait_ge(S["picksT"], 6 * (layer + 1))
                e.wait_ge(S["taken"], LINE0[u] + KEYS)

                def one_hot(i, b):
                    e.wait_ge(S["g_ready"], 4 * i + layer * (T // 4) + b + 1)
                    tt(oh2[:, b], iota[:].unsqueeze(1).broadcast_to([P, 4, P]),
                       picksT[:, 1, bass.ds(16 * i + 4 * b, 4)].unsqueeze(2).broadcast_to([P, 4, P]), ALU.is_equal)
                    for j in range(4):
                        ins = ts(oh1[:, b, j, :], iota[:], picksT[:, 0, bass.ds(16 * i + 4 * b + j, 1)],
                                 picksT[:, 2, bass.ds(16 * i + 4 * b + j, 1)], ALU.is_equal, ALU.mult)
                    ins.then_inc(S["oh_dve"], 1)

                with e.Fori(0, T // 16) as i:
                    one_hot(i, 0)
                    one_hot(i, 2)
                    for b in range(4):
                        e.wait_ge(S["g_ready"], 4 * i + layer * (T // 4) + b + 5)
                        c = C[:, :, bass.ds(16 * i + 4 * b, 4)]
                        tt(c, PS[:, 2 + b, :].rearrange("p (t k) -> p k t", t=4), c, ALU.mult).then_inc(S["g_taken"], 1)

                def c_low(j, up=0):
                    e.wait_ge(S["c_high"], up + layer * KEYS + j + 1)
                    src_ = C[:, j, :] if isinstance(up, int) else C[:, bass.ds(up + j, 1), :]
                    tt(cl_[:, j % 2, :], src_, ch_[:, j % 2, :].bitcast(F32), ALU.subtract).then_inc(S["c_low"], 1)

                e.wait_ge(S["g_taken"], 4 + (layer + 1) * (T // 4))
                c_low(0)
                c_low(1)
                done = 0
                if layer == 0:
                    with e.Fori(0, 4) as i:
                        ch.enter(i, 1)
                        for j in range(24):
                            c_low(j + 2, 24 * i)
                            low(TILE0[v] + j + SLOTS, 24 * i)
                            if j % 2 == 1:
                                row(ROWS + j // 2, mods[:, j // 2:j // 2 + 1], 48 * i)
                        e.wait_ge(S["rows_used"], 12 * i + ROWS + 12)
                        ch(tt(mod[:, bass.ds(12 * i + ROWS, 12)], mods[:], modb[:, bass.ds(12 * i + ROWS, 12)], ALU.add))
                        ch.leave(4)
                    done = 96
                with e.Fori(0, (120 - done) // 6) as i:
                    for j in range(done, done + 6):
                        c_low(j + 2, 6 * i)
                        low(TILE0[v] + j + SLOTS, 6 * i)
                for j in range(120, KEYS):
                    if j + 2 < KEYS:
                        c_low(j + 2)
                    if TILE0[v] + j + SLOTS < TILES:
                        low(TILE0[v] + j + SLOTS)
                if layer == 0:
                    gains(3)
                    gains(4)
                e.wait_ge(S["used"], TILE0[v] + KEYS)
                e.wait_ge(S["c_high"], (layer + 1) * KEYS)
                v_.tensor_copy(y[:, 1, :], PS[:, 4:6, :]).then_inc(S["y_out1"], 1)
                e.wait_ge(S["y_turned"], layer + 1)
                for n in range(NC):
                    ins = residual(PS[:, (0, 1, 6, 7)[n // 2], n % 2 * T:(n % 2 + 1) * T], layer, 5, n)
                ins.then_inc(S["x_new"], NC)
                e.wait_ge(S["x_new"], (2 * layer + 2) * NC)


def tiles(w):
    n = w.shape[1] // P
    return w.reshape(NC, P, n, P).transpose(2, 1, 0, 3).reshape(n, P, D)


def rows(a, chunks):
    return a.reshape(chunks, P).T


def constants():
    ident = np.eye(P, dtype=np.float32)
    axis = ROPE // 2
    half = axis // 2
    turn = np.zeros((ROPE, ROPE), np.float32)
    for a in range(2):
        for j in range(half):
            turn[a * axis + half + j, a * axis + j] = -1.0
            turn[a * axis + j, a * axis + half + j] = 1.0
    pos = np.arange(T)
    inv = (np.float32(10000.0) ** (-np.arange(0, axis, 2, dtype=np.float32) / np.float32(axis))).astype(np.float32)
    ang = np.stack([np.outer((pos // 64).astype(np.float32), inv), np.outer((pos % 64).astype(np.float32), inv)])
    ang = np.repeat(ang[:, None], 2, axis=1).transpose(0, 1, 3, 2).reshape(ROPE, T).astype(np.float32)
    cs = np.stack([np.cos(ang), np.sin(ang)], axis=1).astype(np.float32)
    cnt = np.stack([1.0 / (np.clip(pos + w - w // 2, 0, T) - np.clip(pos - w // 2, 0, T)) for w in WINDOWS])
    cnt = np.broadcast_to(cnt.astype(np.float32), (P, GROUPS, T))
    return ident, turn, cs, cnt


def kernel(**inputs):
    import concourse.bacc as bacc
    from concourse.bass_utils import run_bass_kernel_spmd

    a = {k: np.asarray(v) for k, v in inputs.items()}
    ident, turn, cs, cnt = constants()
    w_in = a["ab_w_in"][0]
    kv0, pool0 = Q_LORA + KV_LORA, Q_LORA + KV_LORA + ROPE
    cin = tiles(a["c_w_in"][0]).reshape(3, NC, P, D).transpose(1, 0, 2, 3).reshape(3 * NC, P, D)
    arrays = {
        "xT": a["x"][0].T.reshape(NC, P, T).transpose(1, 0, 2),
        "ctxT": a["ctx"][0].T.reshape(NC, P, T).transpose(1, 0, 2),
        "c_rows": np.stack([a["c"][0], a["c_ctx"]]),
        "mod_t": a["mod_w"].transpose(0, 2, 1).reshape(LAYERS * ROWS, P, D),
        "mod_b": rows(a["mod_b"], LAYERS * ROWS),
        "norms": np.stack([a["norm_mix"], a["norm_ffn"]]).reshape(2 * LAYERS * NC, P).T.reshape(P, 2, LAYERS, NC),
        "win_t": np.concatenate([tiles(w_in[:, :kv0]), tiles(w_in[:, pool0:])]),
        "wrope": w_in[:, kv0:pool0].reshape(NC, P, ROPE).transpose(1, 0, 2),
        "qa_g": rows(a["q_a_norm"][0], QC),
        "kva_g": rows(a["kv_a_norm"][0], KVC),
        "q_g": a["q_norm"][0][:, None],
        "k_g": a["k_norm"][0][:, None],
        "qb_w": a["q_b_w"][0].reshape(QC, P, -1).transpose(1, 0, 2),
        "kvb_w": a["kv_b_w"][0].reshape(KVC, P, -1).transpose(1, 0, 2),
        "pool_w": a["pool_w"][0].transpose(1, 0, 2),
        "pool_s": rows(a["pool_scale"][0], GROUPS),
        "wout_t": tiles(a["ab_w_out"][0]),
        "cin_t": cin,
        "conv_w": a["c_conv"][0].reshape(3, NC, P).transpose(2, 0, 1),
        "cout_t": tiles(a["c_w_out"][0]),
        "wq_t": np.stack([tiles(a["peer_wq"][i]) for i in range(LAYERS)]),
        "keys_t": a["peer_keys"].transpose(0, 2, 4, 1, 3).reshape(LAYERS, P, HEADS, KEYS),
        "u_t": a["peer_u"].reshape(LAYERS, KEYS, KEYS, NC, P).transpose(0, 1, 4, 3, 2).reshape(LAYERS, KEYS, P, D),
        "v_t": a["peer_v"].reshape(LAYERS, KEYS, P, D),
        "ident_c": ident, "rot_c": turn, "cs_c": cs, "cnt_c": cnt,
    }
    arrays = {k: np.ascontiguousarray(v) for k, v in arrays.items()}
    nc = bacc.Bacc("TRN2", target_bir_lowering=False, num_devices=1,
                   dynamic_dma_scratch_size=1024)
    args = {k: nc.dram_tensor(k, v.shape, F32, kind="ExternalInput").ap() for k, v in arrays.items()}
    args["out"] = nc.dram_tensor("out", (P, NC, T), F32, kind="ExternalOutput").ap()
    hybrid_kernel(nc, **args)
    got = run_bass_kernel_spmd(nc, [arrays], core_ids=[0]).results[0]["out"]
    return got.transpose(2, 1, 0).reshape(1, T, D)
```

```python
from contextlib import ExitStack

import numpy as np

import concourse.bass as bass
from concourse import mybir

F32 = mybir.dt.float32
F32R = mybir.dt.float32r
U32 = mybir.dt.uint32
ALU = mybir.AluOpType
ACT = mybir.ActivationFunctionType
AX = mybir.AxisListType

P = 128
D = 1024
NC = D // P
T = 256
TT = T // P
HEADS = 8
NOPE, ROPE, VH = 64, 32, 64
QH = NOPE + ROPE
Q_LORA, KV_LORA = 384, 256
QC, KVC = Q_LORA // P, KV_LORA // P
GROUPS = 4
WINDOWS = (2, 4, 8, 16)
PAD = 8
KEYS = 128
TOPK = 16
PICKS = HEADS * TOPK
EPS = 1e-6
HROWS = 3 * HEADS
LAYERS = 2
MODS = 6
ROWS = MODS * NC
SLOTS = 3
BY_PE, BY_DVE = 12, 4
LATE = 5 * NC + 1
EARLY = 8
MSLOTS = 4
NEG = -3.0e38

STREAM = [("win", 9), ("wout", NC), ("wq0", HEADS), ("u0", KEYS), ("v0", KEYS),
          ("cin", 3 * NC), ("cout", NC), ("wq1", HEADS), ("u1", KEYS), ("v1", KEYS)]
TILE0, LINE0 = {}, {}
_n = _m = 0
for _name, _count in STREAM:
    TILE0[_name], LINE0[_name] = _n, _m
    _n += _count
    _m += _count if _name[0] != "v" else 0
COUNT = dict(STREAM)
TILES = _n
OUTS = [("ctx", KVC), ("rope", 2), ("qb", HEADS), ("kb", HEADS), ("vb", 4), ("poolw", GROUPS)]
OUT0, _n = {}, 0
for _name, _count in OUTS:
    OUT0[_name] = _n
    _n += _count
TOPK_AT, PICKS_AT = (0, 36), (24, 60)
SECOND_SCORES, EXPS, TURN = 30, (30, 66), 74
MERGE = 78
AFTER = ((), (0, 1), (2,), (3, 4), (5,), (6, 7))
TAIL = 126


def by_pool(j):
    if j < MERGE:
        return j % 3 == 2 and (j < PICKS_AT[0] or TOPK_AT[1] <= j < PICKS_AT[1])
    return j < TAIL and j % 3 == 0


POOL_LOWS = sum(by_pool(j) for j in range(KEYS))


def ring(m):
    return m if m < BY_PE else m - BY_DVE


class Chain:

    def __init__(self, eng, sem):
        self.eng, self.sem, self.n, self.at = eng, sem, 0, None

    def value(self):
        return self.n if self.at is None else self.at + self.n

    def inc(self, ins):
        ins.then_inc(self.sem, 1)
        self.n += 1

    def wait(self):
        self.eng.wait_ge(self.sem, self.value())

    def __call__(self, ins):
        self.inc(ins)
        self.wait()

    def enter(self, i, per):
        self.start, self.per, self.at = self.n, per, i * per

    def leave(self, times):
        assert self.n - self.start == self.per
        self.n, self.at = self.start + times * self.per, None


NORM_BANK = (7, 5, 7, 6, 3, 3, 3)
NORM_CHUNKS = (NC, NC, QC, KVC, NC, NC, NC)


def norms_at(k):
    return [(0, 0, 0), (0, 0, 1), (0, 3, 0), (1, 0, 0), (1, 3, 0)][k]


def hybrid_kernel(nc, xT, ctxT, c_rows, c_cols, mod_first, mod_t, mod_b, norms, win_t, wrope, qa_g, kva_g, q_g, k_g, qb_w, kvb_w, pool_w,
                  pool_s, wout_t, cin_t, conv_w, cout_t, wq_t, keys_t, u_t, v_t, ident_c, rot_c, cs_c, cnt_c, out):
    src = {"win": win_t, "wout": wout_t, "wq0": wq_t[0], "wq1": wq_t[1], "u0": u_t[0], "u1": u_t[1],
           "v0": v_t[0], "v1": v_t[1], "cin": cin_t, "cout": cout_t}
    with ExitStack() as ctx:
        def sb(name, shape, dt=F32):
            return ctx.enter_context(nc.sbuf_tensor(name, shape, dt))

        class Sems(dict):
            def __missing__(self, name):
                self[name] = ctx.enter_context(nc.semaphore(name))
                return self[name]

        S = Sems()
        PS = ctx.enter_context(nc.psum_tensor("PS", [P, 8, 512], F32))
        W = [sb(f"W{i}", [P, D]) for i in range(SLOTS)]
        WH = [sb(f"WH{i}", [P, D], F32R) for i in range(SLOTS)]
        WL = [sb(f"WL{i}", [P, D], F32R) for i in range(SLOTS)]
        x = sb("x", [P, NC, T])
        xh = sb("xh", [P, NC, T], F32R)
        xl = sb("xl", [P, NC, T], F32R)
        ch_ = sb("ch", [P, 2, T], F32R)
        cl_ = sb("cl", [P, 2, T], F32R)
        big = sb("big", [P, KEYS * T])
        C = big[:].rearrange("p (k t) -> p k t", t=T)
        oh1 = sb("oh1", [P, 4, 4, KEYS])
        oh2 = sb("oh2", [P, 4, 4, KEYS])
        ge = sb("ge", [P, 2, T])
        M = [o[:, 2 * j:2 * j + 2].rearrange("p a b c -> p (a b c)") for o in (oh1, oh2) for j in range(2)]

        at = [0]

        def scratch(n, shape_str=None, dt=None, **kw):
            a = big[:, at[0]:at[0] + n]
            at[0] += n
            assert at[0] <= KEYS * T, at[0]
            if dt is not None:
                a = a.bitcast(dt)
            return a.rearrange(shape_str, **kw) if shape_str else a

        sq = scratch(4096)
        hp = scratch(GROUPS * (T + 2 * PAD), "p (g t) -> p g t", g=GROUPS)
        conv_at = at[0]
        ctx_x = scratch(NC * T, "p (c t) -> p c t", t=T)
        xmc = scratch(NC * T, "p (c t) -> p c t", t=T)
        att_at = at[0] - 2 * NC * T
        hq = scratch(QC * T, "p (c t) -> p c t", t=T)
        ckv = scratch(KVC * 2 * T, "p (c t) -> p c t", t=2 * T)
        kro = scratch(2 * T)
        ws = [scratch(T + 2 * PAD) for _ in range(2)]
        pooled = scratch(GROUPS * T, "p (g t) -> p g t", t=T)
        q_all = scratch(HEADS * T, "p (h t) -> p h t", t=T)
        k_all = scratch(HEADS * 2 * T, "p (h t) -> p h t", t=2 * T)
        v_all = scratch(4 * HEADS * VH, "p (k n) -> p k n", k=4)
        qbw = scratch(QC * HEADS * QH, "p (c n) -> p c n", c=QC)
        kvbw = scratch(KVC * HEADS * P, "p (c n) -> p c n", c=KVC)
        plw = scratch(GROUPS * P, "p (g n) -> p g n", g=GROUPS)
        cnt = scratch(GROUPS * T, "p (g t) -> p g t", g=GROUPS)
        wro = scratch(NC * ROPE, "p (c n) -> p c n", c=NC)
        cs = scratch(2 * T, "p (a t) -> p a t", a=2)
        mix_at = at[0]
        mix = scratch(NC * T, "p (c t) -> p c t", t=T)
        rs = scratch(2048)
        hr = scratch(T)
        sel = scratch(2 * HROWS - 1)
        sel_r = scratch(2 * HROWS, "p (s n) -> p s n", s=2)
        diag = scratch(2 * P, "p (b n) -> p b n", b=2)
        xm = mix
        cbx = k_all[:, 0:2, :].rearrange("p h t -> p (h t)")
        dve_rows = big[:, mix_at:mix_at + BY_DVE * D].rearrange("p (k n) -> p k n", n=D)
        m2 = q_all[:].rearrange("p h t -> p (h t)")
        att = big[:, att_at:att_at + 3072]
        qsq = att[:, 0:HEADS * T]
        pe2 = att[:, 0:1024].rearrange("p (b n) -> p b n", b=2)
        pT = att[:, 1024:3072].rearrange("p (b k t) -> p b k t", b=2, k=4)
        at[0] = conv_at
        conv_u = scratch(2 * (T + 2), "p (b t) -> p b t", b=2)
        conv_s = scratch(T)
        conv_h = scratch(2 * 3 * T, "p (b k t) -> p b k t", b=2, k=3)
        at[0] = KEYS * T - 3584
        scratch_at = at[0] // T
        picks = scratch(TT * 3 * PICKS, "p (t k n) -> p t k n", t=TT, k=3)
        sel_v = scratch(2 * TOPK, "p (a k) -> p a k", a=2)
        sel_f = scratch(2 * PICKS, "p (a h k) -> p a h k", a=2, h=HEADS)
        sel_i = scratch(2 * PICKS, "p (a h k) -> p a h k", U32, a=2, h=HEADS)
        rep = scratch(2 * KEYS)
        cand = scratch(TOPK * TOPK)
        top = scratch(PICKS, "p (h k) -> p h k", h=HEADS)
        pos = scratch(PICKS, dt=U32)
        dig = scratch(2 * PICKS, "p (a n) -> p a n", U32, a=2)
        keys = scratch(HEADS * KEYS, "p (h k) -> p h k", h=HEADS)
        q = oh1[:].rearrange("p b j k -> p (b j k)").rearrange("p (h t) -> p h t", t=T)
        eq = oh2[:].rearrange("p b j k -> p (b j k)").rearrange("p (n j) -> p n j", j=TOPK)

        rinv = sb("rinv", [P, T])
        small = sb("small", [P, 64])
        warm = sb("warm", [P, 1])
        eps = sb("eps", [P, 1])
        ones = sb("ones", [P, P])
        zero = sb("zero", [P, P])
        ident = sb("ident", [P, P])
        iota = sb("iota", [P, P])
        cb = sb("cb", [P, D])
        scol = sb("scol", [P, NC, 2])
        mod = sb("mod", [P, LAYERS * ROWS])
        modx = sb("modx", [P, 2 * NC])
        mods = sb("mods", [P, 12])
        modb = sb("modb", [P, LAYERS * ROWS])
        nrm = sb("nrm", [P, 2, LAYERS, NC])
        aff = sb("aff", [P, 5, NC])
        qag = sb("qag", [P, QC])
        kvag = sb("kvag", [P, KVC])
        qg = sb("qg", [P, 2])
        kg = sb("kg", [P, 1])
        pls = sb("pls", [P, GROUPS])
        cvw = sb("cvw", [P, 3, NC])
        rot = sb("rot", [P, ROPE])
        picksT = sb("picksT", [P, 3, T])
        second = sb("second", [P, 2, 4])
        y = big[:, 0:TT * D].rearrange("p (t d) -> p t d", t=TT)

        block = ctx.enter_context(nc.Block())

        @block.sync
        def _(e):
            def weights(name, j, i=None, per=6):
                n = TILE0[name] + j
                if i is None:
                    if n >= SLOTS:
                        e.wait_ge(S["low_ready"], n - SLOTS + 1)
                    s = src[name][j:j + 1]
                else:
                    e.wait_ge(S["low_ready"], per * i + n - SLOTS + 1)
                    s = src[name][bass.ds(per * i + j, 1)]
                e.dma_start(W[n % SLOTS][:], s.rearrange("a p n -> (a p) n")).then_inc(S[f"landed{n % SLOTS}"], 16)

            def rows_tile(m, i=None):
                if i is not None or m >= MSLOTS:
                    e.wait_ge(S["rows_used"], ring(m) - MSLOTS + 1 + (0 if i is None else 12 * i))
                s = (mod_first if m < BY_PE else mod_t)[m:m + 1] if i is None else mod_t[bass.ds(12 * i + m, 1)]
                e.dma_start(M[m % MSLOTS], s.rearrange("a p n -> (a p) n")).then_inc(S[f"rows_landed{m % MSLOTS}"], 16)

            e.dma_start(scol[:], c_cols).then_inc(S["cols_landed"], 16)
            for m in range(MSLOTS):
                rows_tile(m)
            e.dma_start(cb[:], c_rows[0:1, :].broadcast_to([P, D])).then_inc(S["row_landed"], 16)
            e.dma_start(cbx, c_rows[1:2, :].broadcast_to([P, D])).then_inc(S["row_landed"], 16)
            e.dma_start(x[:], xT).then_inc(S["x_landed"], 16)
            for dst, s in [(modb[:], mod_b), (nrm[:], norms), (ident[:], ident_c)]:
                e.dma_start(dst, s).then_inc(S["base"], 16)
            for k in range(BY_DVE):
                s = mod_t[BY_PE + k:BY_PE + k + 1].rearrange("a p n -> (a p) n")
                e.dma_start(dve_rows[:, k, :], s).then_inc(S[f"dve_row{k}"], 16)
                for m in range(MSLOTS + 2 * k, MSLOTS + 2 * k + 2):
                    rows_tile(m)
            for n in range(SLOTS):
                weights("win", n)
            e.dma_start(ctx_x, ctxT).then_inc(S["ctx_landed"], 16)
            ahead = 2
            for n in range(SLOTS, SLOTS + ahead):
                weights("win", n)
            for dst, s in [(wro, wrope), (qag[:], qa_g), (kvag[:], kva_g), (qg[0:QH, 0:1], q_g),
                           (kg[0:QH, :], k_g), (qbw, qb_w), (kvbw, kvb_w), (plw, pool_w), (pls[:], pool_s),
                           (cvw[:], conv_w), (rot[NOPE:QH, :], rot_c), (cs[NOPE:QH, :, :], cs_c), (cnt, cnt_c)]:
                e.dma_start(dst, s).then_inc(S["mixw"], 16)
            for m in range(2 * NC, 2 * NC + MSLOTS):
                rows_tile(m)
            m = 2 * NC + MSLOTS
            follow = {n: 1 for n in range(2 * SLOTS, 2 * SLOTS + COUNT["win"] - 1)}
            follow[14] = LATE - 2 * NC - MSLOTS - (COUNT["win"] - 1)
            for n in range(SLOTS + ahead, TILE0["wq0"] + SLOTS):
                name = "win" if n < TILE0["wout"] else "wout" if n < TILE0["wq0"] else "wq0"
                if QC <= n - SLOTS < QC + KVC:
                    e.wait_ge(S["out_ready"], OUT0["ctx"] + n - SLOTS - QC + 1)
                weights(name, n - TILE0[name])
                for _ in range(follow.get(n, 0)):
                    rows_tile(m)
                    m += 1
            assert m == LATE
            for layer in range(LAYERS):
                wq, u, v = f"wq{layer}", f"u{layer}", f"v{layer}"
                for j in range(SLOTS if layer == 0 else 0, HEADS):
                    weights(wq, j)
                e.wait_ge(S["x_split"], 3 * (layer + 1))
                e.dma_start(keys, keys_t[layer]).then_inc(S["keys_landed"], 16)
                with e.Fori(0, KEYS // 6) as i:
                    for j in range(6):
                        weights(u, j, i)
                for j in range(KEYS // 6 * 6, KEYS):
                    weights(u, j)
                done = 3
                for j in range(done):
                    weights(v, j)
                if layer == 0:
                    e.wait_ge(S["g_ready"], 4 + T // 4)
                    for j in range(12):
                        weights(v, done + j)
                        if j < ROWS - LATE:
                            rows_tile(LATE + j)
                    done += 12
                    with e.Fori(0, 4) as i:
                        for j in range(24):
                            weights(v, done + j, i, 24)
                            if j % 2 == 1:
                                rows_tile(ROWS + j // 2, i)
                    done += 96
                turns = (KEYS - done) // 6
                with e.Fori(0, turns) as i:
                    for j in range(6):
                        weights(v, done + j, i)
                for j in range(done + 6 * turns, KEYS):
                    weights(v, j)
                if layer == 0:
                    with e.Fori(0, NC // 2) as i:
                        for j in range(6):
                            weights("cin", j, i)
                    for j in range(NC):
                        weights("cout", j)
            for c in range(0, NC, 4):
                e.wait_ge(S["x_new"], 3 * NC + c + 4)
                e.dma_start(out[:, c:c + 4, :], x[:, c:c + 4, :]).then_inc(S["stored"], 16)
            e.wait_ge(S["stored"], 32)

        @block.gpsimd
        def _(e):
            nc.gpsimd.memset(ones[:], 1.0).then_inc(S["const"], 1)
            nc.gpsimd.memset(zero[:], 0.0).then_inc(S["const"], 1)
            nc.gpsimd.memset(eps[:], EPS).then_inc(S["const"], 1)
            nc.gpsimd.iota(iota[:], [[1, P]], base=0, channel_multiplier=0,
                           allow_small_or_imprecise_dtypes=True).then_inc(S["const"], 1)
            e.wait_ge(S["const"], 4)
            ch = Chain(e, S["pool_chain"])
            def low(n, up=0):
                e.wait_ge(S["high_ready"], up + n + 1)
                nc.gpsimd.tensor_tensor(WL[n % SLOTS][:], W[n % SLOTS][:], WH[n % SLOTS][:].bitcast(F32), ALU.subtract)\
                    .then_inc(S["pool_low"], 1)

            def add_squares(k):
                for c in range(1, NC - 1):
                    e.wait_ge(S["norm_sq"], sum(NORM_CHUNKS[:k]) + c + 1)
                    ins = nc.gpsimd.tensor_tensor(sq[:, 0:T], sq[:, 0:T], sq[:, c * T:(c + 1) * T], ALU.add)
                    if c < NC - 2:
                        ch(ins)
                ins.then_inc(S["pool_sum"], 1)

            for layer in range(LAYERS):
                add_squares(4 if layer == 0 else 6)
                u = TILE0[f"u{layer}"]

                def one_hot(i, b):
                    e.wait_ge(S["g_ready"], 8 * i + layer * (T // 4) + b + 1)
                    ch.inc(nc.gpsimd.tensor_copy(second[:, b // 2 % 2, :], picksT[:, 1, bass.ds(32 * i + 4 * b, 4)]))
                    ch.wait()
                    e.sem_inc(S["pool_turn"], 1)
                    for j in range(4):
                        ins = nc.gpsimd.tensor_scalar(oh2[:, b % 4, j, :], iota[:], second[:, b // 2 % 2, j:j + 1], None,
                                                      ALU.is_equal)
                    ins.then_inc(S["oh_pool"], 1)

                e.wait_ge(S["x_split"], (3, 6)[layer])
                for j in range(MERGE, scratch_at, 12):
                    nc.gpsimd.memset(C[:, j:j + 12, :], 1.0).then_inc(S["filled"], 1)
                for j in range(MERGE):
                    if by_pool(j):
                        low(u + j + SLOTS)
                e.wait_ge(S["picks_turned"], TT * (layer + 1))
                nc.gpsimd.memset(C[:, scratch_at:, :], 1.0).then_inc(S["filled"], 1)
                e.wait_ge(S["picksT"], 6 * (layer + 1))
                with e.Fori(0, 8) as i:
                    ch.enter(i, 4)
                    one_hot(i, 1)
                    low(u + MERGE + SLOTS, 6 * i)
                    one_hot(i, 3)
                    one_hot(i, 5)
                    low(u + MERGE + 3 + SLOTS, 6 * i)
                    one_hot(i, 7)
                    ch.leave(8)

        @block.tensor
        def _(e):
            mm = nc.tensor.matmul

            def linear(name, j, i=None, per=6, fresh=None, chunks=range(NC), heads=False, conv=False):
                n, line, up = TILE0[name] + j, LINE0[name] + j, 0 if i is None else per * i
                e.wait_ge(S["low_ready"], up + n + 1)
                if line >= 2 or i is not None:
                    e.wait_ge(S["taken"], up + line - 1)
                o = PS[:, line % 2, 0:T]
                h, l = WH[n % SLOTS], WL[n % SLOTS]
                for c in chunks:
                    if fresh is not None:
                        e.wait_ge(S["xl_ready"], fresh * NC + c + 1)
                    if conv:
                        e.wait_ge(S["mix_split"], c + 1)
                    if heads and c == HEADS // 2 - 1:
                        e.wait_ge(S["att_o"], HEADS)
                    mm(o, h[:, c * P:(c + 1) * P], xh[:, c, :], start=c == chunks[0], stop=False)
                    mm(o, h[:, c * P:(c + 1) * P], xl[:, c, :], start=False, stop=False)
                    ins = mm(o, l[:, c * P:(c + 1) * P], xh[:, c, :], start=False, stop=c == chunks[-1])
                ins.then_inc(S["used"], 1)

            def out_bank(name, j):
                n = OUT0[name] + j
                if n >= 2:
                    e.wait_ge(S["out_taken"], n - 1)
                return 4 + n % 2

            def norm(k, width=T):
                n, at_ = NORM_CHUNKS[k], 1024 if k == 3 else 2048 if k == 5 else 0
                for c in range(n):
                    e.wait_ge(S["norm_sq"], sum(NORM_CHUNKS[:k]) + c + 1)
                    ins = mm(PS[:, NORM_BANK[k], 0:width], ones[:], sq[:, at_ + c * width:at_ + (c + 1) * width],
                             start=c == 0, stop=c == n - 1)
                ins.then_inc(S["norm_ss"], 1)

            def norm_summed(k, n, a):
                e.wait_ge(S["sq_sum"], n + 1)
                mm(PS[:, NORM_BANK[k], 0:T], ones[:], a, start=True, stop=True).then_inc(S["norm_ss"], 1)

            def norm_two(k, n):
                e.wait_ge(S["pool_sum"], n + 1)
                o = PS[:, NORM_BANK[k], 0:T]
                mm(o, ones[:], sq[:, 0:T], start=True, stop=False)
                e.wait_ge(S["norm_sq"], sum(NORM_CHUNKS[:k + 1]))
                mm(o, ones[:], sq[:, (NC - 1) * T:NC * T], start=False, stop=True).then_inc(S["norm_ss"], 1)

            e.wait_ge(S["const"], 4)
            e.wait_ge(S["silu"], 1)
            for m in range(BY_PE):
                e.wait_ge(S[f"rows_landed{m % MSLOTS}"], 16 * (m // MSLOTS + 1))
                for a in range(2):
                    c = m % 4 * 2 + a
                    ins = mm(PS[0:2, 2 + m // 4, :], scol[:, c, :], M[m % MSLOTS][:, a * 512:(a + 1) * 512],
                             start=c == 0, stop=c == NC - 1)
                ins.then_inc(S["rows_used"], 1)
                if m == 7:
                    norm_summed(0, 0, hr)
            e.wait_ge(S["base"], 3 * 16)
            for g in range(BY_PE // 4):
                e.wait_ge(S["mod_row"], g + 1)
                for c in range(4 * g, 4 * g + 4):
                    ins = mm(PS[:, 6, 2 * c:2 * c + 2], m2[0:2, c * P:(c + 1) * P], ident[0:2, 0:2], start=True, stop=True)
            ins.then_inc(S["mod_turned"], 1)
            for j in range(COUNT["win"]):
                linear("win", j, fresh=0 if j == 0 else None)
                if j == QC:
                    e.wait_ge(S["ctx_rows"], NC)
                if QC <= j < QC + KVC:
                    e.wait_ge(S[f"landed{j % SLOTS}"], 16 * (j // SLOTS + 1))
                    b = out_bank("ctx", j - QC)
                    for c in range(NC):
                        ins = mm(PS[:, b, 0:T], W[j % SLOTS][:, c * P:(c + 1) * P], xmc[:, c, :], start=c == 0, stop=c == NC - 1)
                    ins.then_inc(S["out_ready"], 1)
                if j == 0:
                    norm_summed(1, 1, diag.rearrange("p b n -> p (b n)"))
                elif j == 3:
                    norm(2)
                elif j == 4:
                    e.wait_ge(S["mixw"], 13 * 16)
                    e.wait_ge(S["xm_whole"], NC)
                    for o, r in enumerate((xmc, xm)):
                        b = out_bank("rope", o)
                        for c in range(NC):
                            ins = mm(PS[NOPE:QH, b, 0:T], wro[:, c, :], r[:, c, :], start=c == 0, stop=c == NC - 1)
                        ins.then_inc(S["out_ready"], 1)
                elif j == 5:
                    norm(3, width=2 * T)
            e.wait_ge(S["out_taken"], OUT0["rope"] + 2)
            mm(PS[NOPE:QH, 3, 0:T], rot[NOPE:QH, :], kro[NOPE:QH, T:], start=True, stop=True).then_inc(S["rot"], 1)
            for h in range(HEADS):
                if h == 0:
                    e.wait_ge(S["norm_out"], 3)
                b = out_bank("qb", h)
                for c in range(QC):
                    ins = mm(PS[0:QH, b, 0:T], qbw[:, c, h * QH:(h + 1) * QH], hq[:, c, :], start=c == 0, stop=c == QC - 1)
                ins.then_inc(S["out_ready"], 1)
            for h in range(HEADS):
                if h == 0:
                    e.wait_ge(S["norm_out"], 4)
                b = out_bank("kb", h)
                for c in range(KVC):
                    ins = mm(PS[0:NOPE, b, :], kvbw[:, c, h * P:h * P + NOPE], ckv[:, c, :], start=c == 0, stop=c == KVC - 1)
                ins.then_inc(S["out_ready"], 1)
                if h == 1:
                    e.wait_ge(S["out_taken"], OUT0["kb"])
                    e.wait_ge(S["taken"], COUNT["win"])
                    e.wait_ge(S["norm_rt"], 4)
                    for j in range(4):
                        ins = mm(PS[NOPE:QH, (6, 7, 0, 1)[j], :], rot[NOPE:QH, :], q_all[NOPE:QH, 2 * j:2 * j + 2, :],
                                 start=True, stop=True)
                    ins.then_inc(S["rot"], 1)
            for kc in range(4):
                b = out_bank("vb", kc)
                for c in range(KVC):
                    ins = mm(PS[:, b, :], ckv[:, c, kc * P:(kc + 1) * P],
                             kvbw[:, c, :].rearrange("p (h n) -> p h n", h=HEADS)[:, :, NOPE:], start=c == 0,
                             stop=c == KVC - 1)
                ins.then_inc(S["out_ready"], 1)
                if kc == 0:
                    e.wait_ge(S["head_sq"], HEADS)
                    o = PS[0:HROWS, 2, 0:T]
                    for h in range(HEADS):
                        mm(o, sel[0:QH, HROWS - 1 - h:2 * HROWS - 1 - h], qsq[0:QH, h * T:(h + 1) * T], start=h == 0, stop=False)
                    for side in range(2):
                        mm(o, sel_r[NOPE:QH, side, :], sq[NOPE:QH, side * T:(side + 1) * T], start=False, stop=False)
                elif kc == 1:
                    e.wait_ge(S["head_sq"], 2 * HEADS)
                    for c in range(2 * HEADS):
                        r = HROWS - 1 - HEADS - c
                        ins = mm(o, sel[0:NOPE, r:r + HROWS], sq[0:NOPE, c * T:(c + 1) * T], start=False, stop=c == 2 * HEADS - 1)
                    ins.then_inc(S["head_ss"], 1)
            e.wait_ge(S["pooled"], GROUPS)
            for g in range(GROUPS):
                b = out_bank("poolw", g)
                mm(PS[:, b, 0:T], plw[:, g, :], pooled[:, g, :], start=True, stop=True).then_inc(S["out_ready"], 1)
            e.wait_ge(S["head_rs"], 1)
            e.wait_ge(S["out_taken"], OUT0["poolw"] + GROUPS)
            for n in range(6):
                if n == 1:
                    e.wait_ge(S["roped"], 2)
                if n >= 3:
                    e.wait_ge(S["head_n"], n - 2)
                for j in range(4):
                    ins = mm(PS[0:QH, (4, 6, 2)[n % 3] + j // 2, j % 2 * T:(j % 2 + 1) * T],
                             ident[0:HROWS, 4 * n + j:4 * n + j + 1].broadcast_to([HROWS, QH]), hr[0:HROWS, :],
                             start=True, stop=True)
                ins.then_inc(S["head_b"], 1)

            def scores(k):
                h, t = divmod(k, TT)
                e.wait_ge(S["head_n"], 3 if k < 2 else 6)
                if k >= 4:
                    e.wait_ge(S["att_exp"], k - 3)
                mm(PS[:, k % 4, :], q_all[0:QH, h, t * P:(t + 1) * P], k_all[0:QH, h, :], start=True,
                   stop=True).then_inc(S["att_s"], 1)

            def turn(k):
                e.wait_ge(S["att_p"], k + 1)
                if k >= 2:
                    e.wait_ge(S["att_c"], k - 1)
                for j in range(4):
                    ins = mm(PS[:, 4 + k % 2, j * P:(j + 1) * P], pe2[:, k % 2, j * P:(j + 1) * P], diag[:, k % 2, :],
                             start=True, stop=True)
                ins.then_inc(S["att_t"], 1)

            def values(h):
                e.wait_ge(S["att_c"], 2 * h + 2)
                if h >= 2:
                    e.wait_ge(S["att_o"], h - 1)
                lo = h % 2 * VH
                for j in range(4):
                    ins = mm(PS[lo:lo + VH, 6 + h % 2, 0:T], v_all[:, j, h * VH:(h + 1) * VH], pT[:, h % 2, j, :],
                             start=j == 0, stop=j == 3)
                ins.then_inc(S["att_v"], 1)

            for k in range(3):
                scores(k)
            for k in range(HEADS * TT):
                if k + 3 < HEADS * TT:
                    scores(k + 3)
                turn(k)
                if k % 2 == 0 and k:
                    values(k // 2 - 1)
            values(HEADS - 1)
            e.wait_ge(S["pool_split"], 1)
            e.wait_ge(S["att_o"], HEADS - 2)
            for n in range(NC):
                linear("wout", n, chunks=(4, 5, 6, 7, 0, 1, 2, 3), heads=n == 0)

            for layer in range(LAYERS):
                if layer == 1:
                    e.wait_ge(S["y_out0"], 2)
                    norm(5)
                    with e.Fori(0, NC // 2) as i:
                        for j in range(6):
                            linear("cin", j, i, fresh=2 if j == 0 else None)
                    for n in range(NC):
                        linear("cout", n, conv=n == 0)
                norm_two(4 if layer == 0 else 6, layer)
                for h in range(HEADS):
                    linear(f"wq{layer}", h, fresh=2 * layer + 1 if h == 0 else None)
                u, v = f"u{layer}", f"v{layer}"

                def key_scores(t):
                    if t:
                        e.wait_ge(S["topk_read"], HEADS * (TT * layer + t))
                    for half in range(2):
                        lo = half * 64
                        for h in range(HEADS):
                            ins = mm(PS[:, 2 + 2 * half + h // 4, h % 4 * P:(h % 4 + 1) * P],
                                     q[lo:lo + 64, h, t * P:(t + 1) * P], keys[lo:lo + 64, h, :], start=True, stop=True)
                    ins.then_inc(S["scores_ready"], 1)

                def blocks(first, last):
                    with e.Fori(0, (last - first) // 6) as i:
                        for j in range(6):
                            linear(u, first + j, i)

                e.wait_ge(S["keys_landed"], 16 * (layer + 1))
                e.wait_ge(S["taken"], LINE0[u])
                key_scores(0)
                blocks(0, SECOND_SCORES)
                key_scores(1)
                blocks(SECOND_SCORES, TURN // 6 * 6)
                for j in range(TURN // 6 * 6, MERGE):
                    if j == TURN:
                        for t in range(TT):
                            e.wait_ge(S["picks"], TT * layer + t + 1)
                            for k in range(3):
                                ins = nc.tensor.transpose(PS[:, 6 + t, k * P:(k + 1) * P], picks[:, t, k, :], ident[:])
                            ins.then_inc(S["picks_turned"], 1)
                    linear(u, j)
                e.wait_ge(S["topk_read"], HEADS * TT * (layer + 1))
                with e.Fori(0, 8) as i:
                    for j in range(6):
                        linear(u, MERGE + j, i)
                        for b in AFTER[j]:
                            n = layer * (T // 4)
                            e.wait_ge(S["g_taken"], 8 * i + n + b + 1)
                            if b % 2 == 0:
                                e.wait_ge(S["oh_dve"], 4 * i + n // 2 + b // 2 + 1)
                            else:
                                e.wait_ge(S["oh_act"], 4 * i + n // 2 + b // 2 + 1)
                                e.wait_ge(S["oh_pool"], 4 * i + n // 2 + b // 2 + 1)
                            for k in range(4):
                                ins = mm(PS[:, 2 + b % 4, k * P:(k + 1) * P], oh2[:, b % 4, k, :], oh1[:, b % 4, k, :],
                                         start=True, stop=True)
                            ins.then_inc(S["g_ready"], 1)
                for j in range(TAIL, KEYS):
                    linear(u, j)
                e.wait_ge(S["g_taken"], 4 + (layer + 1) * (T // 4))
                for b in range(4):
                    mm(PS[:, 2 + b, :], zero[:], x[:, 0:2, :], start=True, stop=False, skip_group_check=True)

                def second_product(j, i=None):
                    n, up = TILE0[v] + j, 0 if i is None else 6 * i
                    e.wait_ge(S["low_ready"], up + n + 1)
                    e.wait_ge(S["c_low"], up + layer * KEYS + j + 1)
                    h, l = WH[n % SLOTS], WL[n % SLOTS]
                    for t in range(TT):
                        for c, w in ((ch_, h), (ch_, l), (cl_, h)):
                            for k in range(2):
                                ins = mm(PS[:, 2 + 2 * t + k, :], c[:, j % 2, t * P:(t + 1) * P], w[:, k * 512:(k + 1) * 512],
                                         start=False, stop=False, skip_group_check=True)
                    ins.then_inc(S["used"], 1)

                with e.Fori(0, 20) as i:
                    for j in range(6):
                        second_product(j, i)
                for j in range(120, KEYS):
                    second_product(j)
                for c in range(NC):
                    if c % 4 == 0:
                        for t in range(TT):
                            e.wait_ge(S[f"y_out{t}"], 2 * layer + c // 4 + 1)
                    b = (0, 1, 6, 7)[c // 2]
                    for t in range(TT):
                        ins = nc.tensor.transpose(PS[:, b, c % 2 * T + t * P:c % 2 * T + (t + 1) * P],
                                                  y[:, t, c * P:(c + 1) * P], ident[:])
                    if c % 2 == 1:
                        ins.then_inc(S["y_turned"], 1)

        @block.scalar
        def _(e):
            act = nc.scalar.activation
            ch = Chain(e, S["act_chain"])

            def high(n, up=0):
                if n >= SLOTS:
                    e.wait_ge(S["used"], up + n - SLOTS + 1)
                e.wait_ge(S[f"landed{n % SLOTS}"], 16 * (n // SLOTS + 1) + (0 if isinstance(up, int) else up_slots[0]))
                act(WH[n % SLOTS][:], W[n % SLOTS][:], ACT.Copy).then_inc(S["high_ready"], 1)

            up_slots = [0]

            def line(name, j, up=0):
                e.wait_ge(S["used"], up + TILE0[name] + j + 1)
                return PS[:, (LINE0[name] + j) % 2, 0:T]

            def ready(name, j):
                n = OUT0[name] + j
                e.wait_ge(S["out_ready"], n + 1)
                return PS[:, 4 + n % 2, :]

            def squares(a, n, at_=0, chunks=NC):
                act(sq[:, at_:at_ + n], a, ACT.Square).then_inc(S["norm_sq"], chunks)

            def root(k, n, width=T):
                e.wait_ge(S["norm_ss"], k + 1)
                if k in (2, 4, 5, 6):
                    e.wait_ge(S["norm_out"], 1 if k == 2 else k)
                r = rs[:, 0:T] if k == 1 else rs[:, 2 * T:4 * T] if k == 3 else rinv[:]
                act(r, PS[:, NORM_BANK[k], 0:width], ACT.Sqrt, bias=eps[:], scale=width / (n * P)).then_inc(S["norm_rt"], 1)

            def shifted(k, which):
                layer, r, _ = norms_at(which)
                for c in range(NC):
                    e.wait_ge(S["norm_t"], k * NC + c + 1)
                    a = layer * ROWS + r * NC + c
                    act(xh[:, c, :], xm[:, c, :], ACT.Identity, bias=mod[:, a:a + 1]).then_inc(S["norm_h"], 1)

            e.wait_ge(S["cols_landed"], 16)
            act(scol[:], scol[:], ACT.Silu).then_inc(S["silu"], 1)
            e.wait_ge(S["row_landed"], 32)
            act(cb[:], cb[:], ACT.Silu).then_inc(S["silu"], 1)
            act(cbx, cbx, ACT.Silu).then_inc(S["silu"], 1)
            e.wait_ge(S["const"], 4)
            e.wait_ge(S["x_landed"], 16)
            squares(x[:], NC * T)
            root(0, NC * T)
            for g in range(BY_PE // 4):
                e.wait_ge(S["rows_used"], 4 * g + 4)
                act(m2[0:2, g * 512:(g + 1) * 512], PS[0:2, 2 + g, :], ACT.Copy).then_inc(S["mod_row"], 1)
            for n in range(SLOTS):
                high(n)
            shifted(0, 0)
            e.wait_ge(S["ctx_landed"], 16)
            squares(ctx_x, NC * T, 2048)
            root(1, NC * T)
            for j in range(COUNT["win"]):
                if QC <= j < QC + KVC:
                    c = j - QC
                    r = ready("ctx", c)[:, 0:T]
                    act(sq[:, 1024 + 2 * c * T:1024 + (2 * c + 1) * T], r, ACT.Square)
                    act(ckv[:, c, 0:T], r, ACT.Copy).then_inc(S["out_taken"], 1)
                high(j + SLOTS)
                r = line("win", j)
                if j < QC:
                    act(sq[:, j * T:(j + 1) * T], r, ACT.Square).then_inc(S["norm_sq"], 1)
                    dst = hq[:, j, :]
                elif j < QC + KVC:
                    act(sq[:, 1024 + (2 * c + 1) * T:1024 + (2 * c + 2) * T], r, ACT.Square).then_inc(S["norm_sq"], 1)
                    dst = ckv[:, c, T:2 * T]
                else:
                    e.wait_ge(S["pad_zero"], 1)
                    dst = hp[:, j - QC - KVC, PAD:PAD + T]
                act(dst, r, ACT.Copy).then_inc(S["taken"], 1)
                if j == 1:
                    for c in range(NC):
                        e.wait_ge(S["ctx_t"], c + 1)
                        act(xmc[:, c, :], xmc[:, c, :], ACT.Identity, bias=modx[:, c:c + 1]).then_inc(S["ctx_rows"], 1)
                elif j == 2:
                    e.wait_ge(S["xl_ready"], NC)
                    for c in range(NC):
                        act(xm[:, c, :], xm[:, c, :], ACT.Identity, bias=mod[:, c:c + 1]).then_inc(S["xm_whole"], 1)
                elif j == 5:
                    root(2, QC * T)
                    e.wait_ge(S["mixw"], 13 * 16)
                    for side in range(2):
                        r = ready("rope", side)[NOPE:QH, 0:T]
                        act(sq[NOPE:QH, side * T:(side + 1) * T], r, ACT.Square)
                        act(kro[NOPE:QH, side * T:(side + 1) * T], r, ACT.Copy, scale=kg[NOPE:QH, :]).then_inc(S["out_taken"], 1)
                elif j == 6:
                    root(3, KVC * 2 * T, width=2 * T)
            for h in range(HEADS):
                r = ready("qb", h)[0:QH, 0:T]
                act(qsq[0:QH, h * T:(h + 1) * T], r, ACT.Square).then_inc(S["head_sq"], 1)
                act(q_all[0:QH, h, :], r, ACT.Copy, scale=qg[0:QH, 0:1]).then_inc(S["out_taken"], 1)
            for h in range(HEADS):
                r = ready("kb", h)[0:NOPE, :]
                act(sq[0:NOPE, h * 2 * T:(h + 1) * 2 * T], r, ACT.Square).then_inc(S["head_sq"], 1)
                act(k_all[0:NOPE, h, :], r, ACT.Copy, scale=kg[0:NOPE, :]).then_inc(S["out_taken"], 1)
            for kc in range(4):
                act(v_all[:, kc, :], ready("vb", kc), ACT.Copy).then_inc(S["out_taken"], 1)
            e.wait_ge(S["head_ss"], 1)
            act(hr[0:HROWS, :], PS[0:HROWS, 2, 0:T], ACT.Sqrt, bias=eps[0:HROWS, :], scale=1.0 / QH).then_inc(S["head_rt"], 1)
            for g in range(GROUPS):
                act(mix[:, 4 + g, :], ready("poolw", g)[:, 0:T], ACT.Copy, scale=pls[:, g:g + 1])\
                    .then_inc(S["out_taken"], 1)

            def exps(k):
                e.wait_ge(S["att_m"], k + 1)
                if k >= 2:
                    e.wait_ge(S["att_t"], k - 1)
                act(pe2[:, k % 2, :], PS[:, k % 4, :], ACT.Exp, bias=small[:, k:k + 1],
                    accum_out=small[:, 16 + k:17 + k]).then_inc(S["att_exp"], 1)

            exps(0)
            for k in range(HEADS * TT):
                if k + 1 < HEADS * TT:
                    exps(k + 1)
                h, t = divmod(k, TT)
                e.wait_ge(S["att_t"], k + 1)
                if h >= 2:
                    e.wait_ge(S["att_v"], h - 1)
                act(pT[:, h % 2, :, t * P:(t + 1) * P],
                    PS[:, 4 + k % 2, :].rearrange("p (j t) -> p j t", j=4), ACT.Copy).then_inc(S["att_c"], 1)

            def sums_squares(name, n):
                e.wait_ge(S["taken"], LINE0[name] + n + 1)
                squares(x[:, n, :], T, n * T, 1)

            act(warm[:], eps[:], ACT.Sqrt)
            for n in range(NC):
                high(TILE0["wout"] + n + SLOTS)
                sums_squares("wout", n)

            for layer in range(LAYERS):
                u, v = f"u{layer}", f"v{layer}"
                if layer == 1:
                    act(warm[:], eps[:], ACT.Sqrt)
                    for c in range(NC):
                        e.wait_ge(S["x_new"], NC + c + 1)
                        squares(x[:, c, :], T, 2048 + c * T, 1)
                    root(5, NC * T)
                    shifted(2, 3)
                    with e.Fori(0, NC // 2) as i:
                        up_slots[0] = 32 * i
                        for j in range(6):
                            n, k = divmod(j, 3)
                            if k < 2:
                                high(TILE0["cin"] + j + SLOTS, 6 * i)
                            if k == 0:
                                e.wait_ge(S["conv_taken"], 2 * i + n + 1)
                            act(conv_h[:, n, k, :], line("cin", j, 6 * i), ACT.Copy).then_inc(S["taken"], 1)
                            if k == 2:
                                high(TILE0["cin"] + j + SLOTS, 6 * i)
                    e.wait_ge(S["used"], TILE0["cout"])
                    for c in range(NC):
                        e.wait_ge(S["conv_taken"], c + 3)
                        act(xh[:, c, :], mix[:, c, :], ACT.Copy).then_inc(S["mix_h"], 1)
                    act(warm[:], eps[:], ACT.Sqrt)
                    for n in range(NC):
                        high(TILE0["cout"] + n + SLOTS)
                        sums_squares("cout", n)
                root(4 if layer == 0 else 6, NC * T)
                shifted(1 if layer == 0 else 3, 2 if layer == 0 else 4)
                for h in range(HEADS):
                    high(TILE0[f"wq{layer}"] + h + SLOTS)
                    act(q[:, h, :], line(f"wq{layer}", h), ACT.Copy).then_inc(S["taken"], 1)

                def blocks(first, last):
                    act(warm[:], eps[:], ACT.Gelu)
                    with e.Fori(0, (last - first) // 6) as i:
                        up_slots[0] = 32 * i
                        for j in range(6):
                            high(TILE0[u] + first + j + SLOTS, 6 * i)
                            act(C[:, bass.ds(6 * i + first + j, 1), :], line(u, first + j, 6 * i), ACT.Gelu)\
                                .then_inc(S["taken"], 1)

                def gate_exp(t):
                    e.wait_ge(S["gate_d"], TT * layer + t + 1)
                    act(picks[:, t, 2, :], top, ACT.Exp).then_inc(S["gate_e"], 1)

                blocks(0, EXPS[0])
                gate_exp(0)
                blocks(EXPS[0], EXPS[1])
                gate_exp(1)
                blocks(EXPS[1], MERGE)

                def merged(j, up=0):
                    high(TILE0[u] + j + SLOTS, up)
                    e.wait_ge(S["ge_used"], up + layer * (KEYS - MERGE) + j - MERGE + 1)
                    act(ge[:, j % 2, :], line(u, j, up), ACT.Gelu).then_inc(S["taken"], 1)

                def one_hot(i, b):
                    e.wait_ge(S["g_ready"], 8 * i + layer * (T // 4) + b + 1)
                    for j in range(4):
                        ins = act(oh1[:, b % 4, j, :], iota[:], ACT.Abs, scale=-1.0,
                                  bias=picksT[:, 0, bass.ds(32 * i + 4 * b + j, 1)])
                    ch(ins)
                    for j in range(4):
                        ins = act(oh1[:, b % 4, j, :], oh1[:, b % 4, j, :], ACT.Relu, scale=-1.0,
                                  bias=picksT[:, 2, bass.ds(32 * i + 4 * b + j, 1)])
                    ins.then_inc(S["oh_act"], 1)

                e.wait_ge(S["picksT"], 6 * (layer + 1))
                with e.Fori(0, 8) as i:
                    ch.enter(i, 4)
                    up_slots[0] = 32 * i
                    one_hot(i, 1)
                    merged(MERGE, 6 * i)
                    one_hot(i, 3)
                    merged(MERGE + 1, 6 * i)
                    one_hot(i, 5)
                    merged(MERGE + 2, 6 * i)
                    merged(MERGE + 3, 6 * i)
                    one_hot(i, 7)
                    merged(MERGE + 4, 6 * i)
                    merged(MERGE + 5, 6 * i)
                    ch.leave(8)
                for j in range(TAIL, KEYS):
                    merged(j)

                def c_high(j, up=0):
                    if j >= 2:
                        e.wait_ge(S["used"], up + TILE0[v] + j - 1)
                    src_ = C[:, j, :] if isinstance(up, int) else C[:, bass.ds(up + j, 1), :]
                    act(ch_[:, j % 2, :], src_, ACT.Copy).then_inc(S["c_high"], 1)

                e.wait_ge(S["g_taken"], 4 + (layer + 1) * (T // 4))
                e.wait_ge(S["ge_used"], (layer + 1) * (KEYS - MERGE) + 2)
                c_high(0)
                c_high(1)
                with e.Fori(0, 20) as i:
                    up_slots[0] = 32 * i
                    for j in range(6):
                        c_high(j + 2, 6 * i)
                        high(TILE0[v] + j + SLOTS, 6 * i)
                for j in range(120, KEYS):
                    if j + 2 < KEYS:
                        c_high(j + 2)
                    if j < KEYS - 1 and TILE0[v] + j + SLOTS < TILES:
                        high(TILE0[v] + j + SLOTS)
                e.wait_ge(S["used"], TILE0[v] + KEYS)
                e.wait_ge(S["c_low"], (layer + 1) * KEYS)
                for k in range(2):
                    act(y[:, 0, k * 512:(k + 1) * 512], PS[:, 2 + k, :], ACT.Copy).then_inc(S["y_out0"], 1)
                if layer < LAYERS - 1:
                    high(TILE0[v] + KEYS - 1 + SLOTS)

        @block.vector
        def _(e):
            v_ = nc.vector
            ch = Chain(e, S["dve_chain"])
            tt, stt, ts = v_.tensor_tensor, v_.scalar_tensor_tensor, v_.tensor_scalar

            def low(n, up=0):
                e.wait_ge(S["high_ready"], up + n + 1)
                tt(WL[n % SLOTS][:], W[n % SLOTS][:], WH[n % SLOTS][:].bitcast(F32), ALU.subtract).then_inc(S["low_ready"], 1)

            def row(m, dst=None, i=None):
                e.wait_ge(S[f"rows_landed{m % MSLOTS}"], 16 * (ring(m) // MSLOTS + 1) + (0 if i is None else i))
                w = M[m % MSLOTS]
                v_.tensor_tensor_reduce(out=w, in0=w, in1=cb[:], scale=1.0, scalar=0.0, op0=ALU.mult, op1=ALU.add,
                                        accum_out=mod[:, m:m + 1] if dst is None else dst).then_inc(S["rows_used"], 1)

            def add_bias(first, last):
                e.wait_ge(S["rows_used"], ring(last))
                ch(tt(mod[:, first:last], mod[:, first:last], modb[:, first:last], ALU.add))

            def line(name, j):
                e.wait_ge(S["used"], TILE0[name] + j + 1)
                return PS[:, (LINE0[name] + j) % 2, 0:T]

            def mrow(layer, k, col=0):
                a = layer * ROWS + k * NC
                return modx[:, k * NC:(k + 1) * NC] if col else mod[:, a:a + NC]

            def gains(k):
                layer, r, col = norms_at(k)
                ch(stt(aff[:, k, :], mrow(layer, r + 1, col), 1.0, nrm[:, 0 if r == 0 else 1, layer, :], ALU.add, ALU.mult))

            def norm(k, src_, dst, which=None, gain=None, chunks=NC, width=T):
                e.wait_ge(S["norm_rt"], k + 1)
                r = rs[:, 0:T] if k == 1 else rs[:, 2 * T:4 * T] if k == 3 else rinv[:]
                ch(v_.reciprocal(r, r))
                for c in range(chunks):
                    g = gain[:, c:c + 1] if which is None else aff[:, which, c:c + 1]
                    ch.inc(stt(dst[:, c, :], src_[:, c, :], g, r, ALU.mult, ALU.mult))
                ch.wait()
                if which is not None:
                    layer, r_, col = norms_at(which)
                    for c in range(chunks):
                        ch.inc(ts(dst[:, c, :], dst[:, c, :], mrow(layer, r_, col)[:, c:c + 1], None, ALU.add))
                    ch.wait()
                e.nop().then_inc(S["norm_out"], 1)

            def inverse_root(k):
                e.wait_ge(S["norm_rt"], k + 1)
                ch(v_.reciprocal(rinv[:], rinv[:]))

            def norm_split(k, n, which, inverse=True):
                layer, r_, _ = norms_at(which)
                shift = mrow(layer, r_)
                if inverse:
                    inverse_root(k)
                for c in range(NC + 2):
                    if c < NC:
                        stt(xm[:, c, :], x[:, c, :], aff[:, which, c:c + 1], rinv[:], ALU.mult, ALU.mult)\
                            .then_inc(S["norm_t"], 1)
                    if c >= 2:
                        b = c - 2
                        e.wait_ge(S["norm_h"], n * NC + b + 1)
                        stt(xl[:, b, :], xm[:, b, :], shift[:, b:b + 1], xh[:, b, :].bitcast(F32), ALU.add, ALU.subtract)\
                            .then_inc(S["xl_ready"], 1)
                e.wait_ge(S["xl_ready"], (n + 1) * NC)
                e.nop().then_inc(S["x_split"], 1)
                e.nop().then_inc(S["norm_out"], 1)

            def split(a, first, last, done):
                ch(v_.tensor_copy(xh[:, first:last, :], a[:, first:last, :]))
                ins = tt(xl[:, first:last, :], a[:, first:last, :], xh[:, first:last, :].bitcast(F32), ALU.subtract)
                ins.then_inc(done, 1)

            def residual(a, layer, r, n):
                return stt(x[:, n, :], a, mrow(layer, r)[:, n:n + 1], x[:, n, :], ALU.mult, ALU.add)

            v_.memset(small[:, 63:64], 0.0).then_inc(S["g_ready"], 4)
            v_.memset(small[:, 62:63], 0.0).then_inc(S["g_taken"], 4)
            v_.memset(small[:, 61:62], 0.0).then_inc(S["conv_taken"], 2)
            v_.memset(small[:, 60:61], 0.0).then_inc(S["ge_used"], 2)
            v_.memset(hp, 0.0)
            ch(v_.memset(sel, 0.0))
            ch(v_.memset(sel_r, 0.0))
            v_.memset(sel[:, HROWS - 1:HROWS], 1.0)
            pairs = sel_r.rearrange("p s (h k) -> p s h k", k=2)[:, :, HEADS // 2:, :]
            v_.memset(pairs[:, 0, :, 0], 1.0)
            v_.memset(pairs[:, 1, :, 1], 1.0).then_inc(S["pad_zero"], 1)
            def sum_chunks(dst, a, squares_before):
                e.wait_ge(S["norm_sq"], squares_before + NC)
                v_.tensor_reduce(dst, a.rearrange("p (c t) -> p t c", t=T), AX.X, ALU.add).then_inc(S["sq_sum"], 1)

            e.wait_ge(S["silu"], 3)
            for k in range(BY_DVE):
                e.wait_ge(S[f"dve_row{k}"], 16)
                for cond, dst in ((cbx, modx[:, BY_PE + k:BY_PE + k + 1]), (cb[:], mod[:, BY_PE + k:BY_PE + k + 1])):
                    ch(v_.tensor_tensor_reduce(out=k_all[:, 2:4, :].rearrange("p h t -> p (h t)"), in0=dve_rows[:, k, :],
                                               in1=cond, scale=1.0, scalar=0.0, op0=ALU.mult, op1=ALU.add, accum_out=dst))
                if k == 0:
                    sum_chunks(hr, sq[:, 0:NC * T], 0)
            inverse_root(0)
            low(0)
            low(1)
            e.wait_ge(S["base"], 3 * 16)
            e.wait_ge(S["mod_turned"], 1)
            both = PS[:, 6, 0:2 * BY_PE].rearrange("p (c k) -> p k c", k=2)

            def turned_rows(dst, turned):
                ch.inc(tt(dst[:, 0:BY_PE], turned, modb[:, 0:BY_PE], ALU.add))
                ch(tt(dst[:, BY_PE:2 * NC], dst[:, BY_PE:2 * NC], modb[:, BY_PE:2 * NC], ALU.add))

            turned_rows(mod, both[:, 0, :])
            gains(0)
            norm_split(0, 0, 0, inverse=False)
            sum_chunks(diag.rearrange("p b n -> p (b n)"), sq[:, 2048:2048 + NC * T], NC)
            low(2)
            turned_rows(modx, both[:, 1, :])
            gains(1)
            low(SLOTS)
            e.wait_ge(S["norm_rt"], 2)
            ch(v_.reciprocal(rs[:, 0:T], rs[:, 0:T]))
            for c in range(NC):
                stt(xmc[:, c, :], ctx_x[:, c, :], aff[:, 1, c:c + 1], rs[:, 0:T], ALU.mult, ALU.mult).then_inc(S["ctx_t"], 1)
            e.wait_ge(S["ctx_t"], NC)
            e.nop().then_inc(S["norm_out"], 1)
            for n in range(COUNT["win"]):
                if n:
                    low(n + SLOTS)
                row(2 * NC + n)
                if n == 5:
                    norm(2, hq, hq, gain=qag, chunks=QC)
                elif n == 6:
                    norm(3, ckv, ckv, gain=kvag, chunks=KVC, width=2 * T)
            add_bias(2 * NC, 3 * NC)
            sin, cos = cs[NOPE:QH, 1, :], cs[NOPE:QH, 0, :]
            e.wait_ge(S["mixw"], 13 * 16)
            e.wait_ge(S["rot"], 1)
            kr = kro[NOPE:QH, T:]
            ch(tt(rs[NOPE:QH, 0:T], PS[NOPE:QH, 3, 0:T], sin, ALU.mult))
            ch(tt(kr, kr, cos, ALU.mult))
            tt(kr, kr, rs[NOPE:QH, 0:T], ALU.add).then_inc(S["roped"], 1)
            e.wait_ge(S["roped"], 1)
            ch(v_.tensor_copy(k_all[NOPE:QH], kro[NOPE:QH, :].unsqueeze(1).broadcast_to([ROPE, HEADS, 2 * T])))
            e.wait_ge(S["taken"], COUNT["win"])
            for g, w in enumerate(WINDOWS):
                cur, n, size = hp[:, g, :], T + 2 * PAD, 1
                k = 0
                while size < w:
                    n -= size
                    ch(tt(ws[k % 2][:, 0:n], cur[:, 0:n], cur[:, size:size + n], ALU.add))
                    cur = ws[k % 2]
                    k += 1
                    size *= 2
                a = PAD - w // 2
                ch(tt(pooled[:, g, :], cur[:, a:a + T], cnt[:, g, :], ALU.mult))
                ch(tt(pooled[:, g, :], pooled[:, g, :], hp[:, g, PAD:PAD + T], ALU.subtract))
            e.nop().then_inc(S["pooled"], GROUPS)
            e.wait_ge(S["rot"], 2)
            for n, b in enumerate((6, 0)):
                a = q_all[NOPE:QH, 4 * n:4 * n + 4, :]
                t2 = rs[NOPE:QH, 0:4 * T].rearrange("p (h t) -> p h t", t=T)
                ch(tt(t2, PS[NOPE:QH, b:b + 2, :].rearrange("p b (h t) -> p (b h) t", t=T),
                      sin.unsqueeze(1).broadcast_to([ROPE, 4, T]), ALU.mult))
                ch(tt(a, a, cos.unsqueeze(1).broadcast_to([ROPE, 4, T]), ALU.mult))
                ch(tt(a, a, t2, ALU.add))
            e.nop().then_inc(S["roped"], 1)
            for m in range(3 * NC + 1, 3 * NC + 1 + EARLY):
                row(m)
            e.wait_ge(S["head_rt"], 1)
            ch(v_.reciprocal(hr[0:HROWS, :], hr[0:HROWS, :]))
            ts(hr[0:HEADS, :], hr[0:HEADS, :], float(QH) ** -0.5, None, ALU.mult).then_inc(S["head_rs"], 1)
            e.wait_ge(S["out_taken"], OUT0["poolw"] + GROUPS)
            split(mix, 4, 8, S["pool_split"])
            for n in range(6):
                e.wait_ge(S["head_b"], n + 1)
                a = q_all[0:QH, 4 * n:4 * n + 4, :] if n < 2 else k_all[0:QH, 2 * (n - 2):2 * (n - 1), :]
                a = a.rearrange("p h t -> p (h t)")
                b = (4, 6, 2)[n % 3]
                tt(a, a, PS[0:QH, b:b + 2, :].rearrange("p b t -> p (b t)"), ALU.mult).then_inc(S["head_n"], 1)

            def maxes(k):
                e.wait_ge(S["att_s"], k + 1)
                v_.tensor_reduce(small[:, k:k + 1], PS[:, k % 4, :], AX.X, ALU.max, negate=True).then_inc(S["att_m"], 1)

            def head_out(h):
                e.wait_ge(S["att_v"], h + 1)
                lo = h % 2 * VH
                a, hi = PS[lo:lo + VH, 6 + h % 2, 0:T], xh[lo:lo + VH, h // 2, :]
                ch(v_.tensor_copy(hi, a))
                tt(xl[lo:lo + VH, h // 2, :], a, hi.bitcast(F32), ALU.subtract).then_inc(S["att_o"], 1)
                e.wait_ge(S["att_o"], h + 1)

            maxes(0)
            maxes(1)
            for k in range(HEADS * TT):
                if k + 2 < HEADS * TT:
                    maxes(k + 2)
                e.wait_ge(S["att_exp"], k + 1)
                ch(v_.reciprocal(small[:, 32 + k % 8:33 + k % 8], small[:, 16 + k:17 + k]))
                ts(diag[:, k % 2, :], ident[:], small[:, 32 + k % 8:33 + k % 8], None, ALU.mult).then_inc(S["att_p"], 1)
                if k % 2 == 1 and k >= 3:
                    head_out(k // 2 - 1)
                if k % 2 == 0 and 3 * NC + 1 + EARLY + k // 2 < LATE:
                    row(3 * NC + 1 + EARLY + k // 2)
            head_out(HEADS - 1)
            e.nop().then_inc(S["x_split"], 1)
            for n in range(NC):
                residual(line("wout", n), 0, 2, n).then_inc(S["taken"], 1)
                low(TILE0["wout"] + n + SLOTS)
            e.wait_ge(S["taken"], LINE0["wout"] + NC)
            e.nop().then_inc(S["x_new"], NC)
            add_bias(3 * NC, 5 * NC)
            gains(2)

            for layer in range(LAYERS):
                u, v = f"u{layer}", f"v{layer}"
                if layer == 1:
                    norm_split(5, 2, 3)
                    ch(v_.memset(conv_u, 0.0))
                    with e.Fori(0, NC // 2) as i:
                        ch.enter(i, 8)
                        for n in range(2):
                            for k in range(2):
                                low(TILE0["cin"] + 3 * n + k + SLOTS, 6 * i)
                            e.wait_ge(S["taken"], 6 * i + LINE0["cin"] + 3 * n + 3)
                            h_ = conv_h[:, n]
                            u_ = conv_u[:, n]
                            ch(tt(u_[:, 1:T + 1], h_[:, 1, :], h_[:, 2, :], ALU.mult))
                            ch(ts(conv_s, u_[:, 0:T], cvw[:, 0, bass.ds(2 * i + n, 1)], None, ALU.mult))
                            ch(stt(conv_s, u_[:, 1:T + 1], cvw[:, 1, bass.ds(2 * i + n, 1)], conv_s, ALU.mult, ALU.add))
                            ch(stt(conv_s, u_[:, 2:T + 2], cvw[:, 2, bass.ds(2 * i + n, 1)], conv_s, ALU.mult, ALU.add))
                            tt(mix[:, bass.ds(2 * i + n, 1), :], h_[:, 0, :], conv_s, ALU.mult).then_inc(S["conv_taken"], 1)
                            e.wait_ge(S["conv_taken"], 2 * i + n + 3)
                            low(TILE0["cin"] + 3 * n + 2 + SLOTS, 6 * i)
                        ch.leave(NC // 2)
                    for c in range(NC):
                        e.wait_ge(S["mix_h"], c + 1)
                        tt(xl[:, c, :], mix[:, c, :], xh[:, c, :].bitcast(F32), ALU.subtract).then_inc(S["mix_split"], 1)
                    e.wait_ge(S["mix_split"], NC)
                    e.nop().then_inc(S["x_split"], 1)
                    for n in range(NC):
                        residual(line("cout", n), 1, 2, n).then_inc(S["taken"], 1)
                        low(TILE0["cout"] + n + SLOTS)
                    e.wait_ge(S["taken"], LINE0["cout"] + NC)
                    e.nop().then_inc(S["x_new"], NC)
                if layer == 0:
                    norm_split(4, 1, 2)
                else:
                    norm_split(6, 3, 4)
                for h in range(HEADS):
                    low(TILE0[f"wq{layer}"] + h + SLOTS)

                def key_topk(t, h, half):
                    if h == 0 and half == 0:
                        e.wait_ge(S["scores_ready"], TT * layer + t + 1)
                    s = PS[:, 2 + 2 * half + h // 4, h % 4 * P:(h % 4 + 1) * P]
                    lo, hi = sel_v[:, half, 0:8], sel_v[:, half, 8:16]
                    ch(v_.max(lo, s))
                    ch.inc(v_.max_index(sel_i[:, half, h, 0:8], lo, s))
                    ch(v_.match_replace(rep[:, 0:KEYS], lo, s, NEG))
                    ch(v_.max(hi, rep[:, 0:KEYS]))
                    ch(v_.max_index(sel_i[:, half, h, 8:16], hi, rep[:, 0:KEYS]))

                def pair_topk(h):
                    e.nop().then_inc(S["topk_read"], 1)
                    ch(tt(cand.rearrange("p (a b) -> p a b", a=TOPK), sel_v[:, 0, :].unsqueeze(2).broadcast_to([P, TOPK, TOPK]),
                          sel_v[:, 1, :].unsqueeze(1).broadcast_to([P, TOPK, TOPK]), ALU.add))
                    ps = pos[:, h * TOPK:(h + 1) * TOPK]
                    ch(v_.max(top[:, h, 0:8], cand))
                    ch.inc(v_.max_index(ps[:, 0:8], top[:, h, 0:8], cand))
                    ch(v_.match_replace(rep, top[:, h, 0:8], cand, NEG))
                    ch(v_.max(top[:, h, 8:16], rep))
                    ch(v_.max_index(ps[:, 8:16], top[:, h, 8:16], rep))

                def find(t, part):
                    e4 = eq.rearrange("p (h k) j -> p h k j", h=HEADS)
                    half = 0 if part < 6 else 1
                    if part == 0:
                        ch(v_.tensor_copy(small[:, 0:8], top[:, :, 0]))
                        tt(top, top, small[:, 0:8].unsqueeze(2).broadcast_to([P, HEADS, TOPK]), ALU.subtract)\
                            .then_inc(S["gate_d"], 1)
                        ch(v_.tensor_copy(sel_f, sel_i))
                        ch(ts(dig[:, 0, :], pos, 4, None, ALU.logical_shift_right))
                        ch(ts(dig[:, 1, :], pos, 15, None, ALU.bitwise_and))
                    elif part in (1, 6):
                        ch(tt(eq, dig[:, half, :].unsqueeze(2).broadcast_to([P, PICKS, TOPK]),
                              iota[:, 0:TOPK].unsqueeze(1).broadcast_to([P, PICKS, TOPK]), ALU.is_equal))
                    elif part in (3, 8):
                        ch(tt(e4, e4, sel_f[:, half].unsqueeze(2).broadcast_to([P, HEADS, TOPK, TOPK]), ALU.mult))
                    elif part in (4, 10):
                        ch(v_.tensor_reduce(picks[:, t, half, :], eq, AX.X, ALU.add))
                    elif part == 12:
                        e.wait_ge(S["gate_e"], TT * layer + t + 1)
                        g = picks[:, t, 2, :].rearrange("p (h k) -> p h k", h=HEADS)
                        ch(v_.tensor_reduce(small[:, 8:16], g, AX.X, ALU.add))
                        ch(v_.reciprocal(small[:, 16:24], small[:, 8:16]))
                        tt(g, g, small[:, 16:24].unsqueeze(2).broadcast_to([P, HEADS, TOPK]), ALU.mult)\
                            .then_inc(S["picks"], 1)

                def low_of_pool(j, i=0):
                    e.wait_ge(S["low_ready"], 6 * i + TILE0[u] + j + SLOTS)
                    done = layer * POOL_LOWS + sum(by_pool(k) for k in range(j + 1))
                    e.wait_ge(S["pool_low"], 2 * i + done)
                    e.nop().then_inc(S["low_ready"], 1)

                for j in range(MERGE):
                    if not by_pool(j):
                        low(TILE0[u] + j + SLOTS)
                    for t in range(TT):
                        h, part = divmod(j - TOPK_AT[t], 3)
                        if 0 <= h < HEADS:
                            if part < 2:
                                key_topk(t, h, part)
                            else:
                                pair_topk(h)
                        if 0 <= j - PICKS_AT[t] <= 12:
                            find(t, j - PICKS_AT[t])
                    if by_pool(j):
                        low_of_pool(j)
                    if j == TURN:
                        for t in range(TT):
                            e.wait_ge(S["picks_turned"], TT * layer + t + 1)
                            for k in range(3):
                                v_.tensor_copy(picksT[:, k, t * P:(t + 1) * P], PS[:, 6 + t, k * P:(k + 1) * P])\
                                    .then_inc(S["picksT"], 1)
                e.wait_ge(S["picksT"], 6 * (layer + 1))
                fills = len(range(MERGE, scratch_at, 12)) + 1
                e.wait_ge(S["filled"], fills * (layer + 1))
                e.wait_ge(S["taken"], LINE0[u] + MERGE)

                def one_hot(i, b):
                    e.wait_ge(S["g_ready"], 8 * i + layer * (T // 4) + b + 1)
                    tt(oh2[:, b % 4], iota[:].unsqueeze(1).broadcast_to([P, 4, P]),
                       picksT[:, 1, bass.ds(32 * i + 4 * b, 4)].unsqueeze(2).broadcast_to([P, 4, P]), ALU.is_equal)
                    for j in range(4):
                        ins = ts(oh1[:, b % 4, j, :], iota[:], picksT[:, 0, bass.ds(32 * i + 4 * b + j, 1)],
                                 picksT[:, 2, bass.ds(32 * i + 4 * b + j, 1)], ALU.is_equal, ALU.mult)
                    ins.then_inc(S["oh_dve"], 1)

                def times_block(j, i=None):
                    up = 0 if i is None else 6 * i
                    e.wait_ge(S["taken"], up + LINE0[u] + j + 1)
                    groups = T // 4 if i is None else 8 * i + sum(map(len, AFTER[:j - MERGE]))
                    e.wait_ge(S["g_taken"], groups + layer * (T // 4) + 4)
                    c = C[:, j, :] if i is None else C[:, bass.ds(up + j, 1), :]
                    tt(c, ge[:, j % 2, :], c, ALU.mult).then_inc(S["ge_used"], 1)

                def times_gates(i, b, j):
                    e.wait_ge(S["ge_used"], 6 * i + layer * (KEYS - MERGE) + j + 3)
                    e.wait_ge(S["g_ready"], 8 * i + layer * (T // 4) + b + 5)
                    c = C[:, :, bass.ds(32 * i + 4 * b, 4)]
                    tt(c, PS[:, 2 + b % 4, :].rearrange("p (t k) -> p k t", t=4), c, ALU.mult).then_inc(S["g_taken"], 1)

                with e.Fori(0, 8) as i:
                    one_hot(i, 0)
                    for j in range(6):
                        if j in (0, 2, 3):
                            one_hot(i, (2, None, 4, 6)[j])
                        if not by_pool(MERGE + j):
                            low(TILE0[u] + MERGE + j + SLOTS, 6 * i)
                        times_block(MERGE + j, i)
                        for b in AFTER[j]:
                            times_gates(i, b, j)
                        if by_pool(MERGE + j):
                            low_of_pool(MERGE + j, i)
                for j in range(TAIL, KEYS):
                    low(TILE0[u] + j + SLOTS)
                    times_block(j)

                def c_low(j, up=0):
                    e.wait_ge(S["c_high"], up + layer * KEYS + j + 1)
                    src_ = C[:, j, :] if isinstance(up, int) else C[:, bass.ds(up + j, 1), :]
                    tt(cl_[:, j % 2, :], src_, ch_[:, j % 2, :].bitcast(F32), ALU.subtract).then_inc(S["c_low"], 1)

                c_low(0)
                c_low(1)
                done = 0
                if layer == 0:
                    for j in range(12):
                        c_low(j + 2)
                        low(TILE0[v] + j + SLOTS)
                        if j < ROWS - LATE:
                            row(LATE + j)
                    add_bias(5 * NC, ROWS)
                    with e.Fori(0, 4) as i:
                        ch.enter(i, 1)
                        for j in range(12, 36):
                            c_low(j + 2, 24 * i)
                            low(TILE0[v] + j + SLOTS, 24 * i)
                            if j % 2 == 1:
                                row(ROWS + j // 2 - 6, mods[:, j // 2 - 6:j // 2 - 5], 48 * i)
                        e.wait_ge(S["rows_used"], 12 * i + ring(ROWS) + 12)
                        ch(tt(mod[:, bass.ds(12 * i + ROWS, 12)], mods[:], modb[:, bass.ds(12 * i + ROWS, 12)], ALU.add))
                        ch.leave(4)
                    done = 108
                    gains(3)
                    gains(4)
                with e.Fori(0, (120 - done) // 6) as i:
                    for j in range(done, done + 6):
                        c_low(j + 2, 6 * i)
                        low(TILE0[v] + j + SLOTS, 6 * i)
                for j in range(120, KEYS):
                    if j + 2 < KEYS:
                        c_low(j + 2)
                    if j < KEYS - 1 and TILE0[v] + j + SLOTS < TILES:
                        low(TILE0[v] + j + SLOTS)
                e.wait_ge(S["used"], TILE0[v] + KEYS)
                e.wait_ge(S["c_high"], (layer + 1) * KEYS)
                for k in range(2):
                    v_.tensor_copy(y[:, 1, k * 512:(k + 1) * 512], PS[:, 4 + k, :]).then_inc(S["y_out1"], 1)
                for n in range(NC):
                    if n % 2 == 0:
                        e.wait_ge(S["y_turned"], layer * NC // 2 + n // 2 + 1)
                    residual(PS[:, (0, 1, 6, 7)[n // 2], n % 2 * T:(n % 2 + 1) * T], layer, 5, n).then_inc(S["x_new"], 1)
                if layer < LAYERS - 1:
                    low(TILE0[v] + KEYS - 1 + SLOTS)
                e.wait_ge(S["x_new"], (2 * layer + 2) * NC)


def tiles(w):
    n = w.shape[1] // P
    return w.reshape(NC, P, n, P).transpose(2, 1, 0, 3).reshape(n, P, D)


def rows(a, chunks):
    return a.reshape(chunks, P).T


def constants():
    ident = np.eye(P, dtype=np.float32)
    axis = ROPE // 2
    half = axis // 2
    turn = np.zeros((ROPE, ROPE), np.float32)
    for a in range(2):
        for j in range(half):
            turn[a * axis + half + j, a * axis + j] = -1.0
            turn[a * axis + j, a * axis + half + j] = 1.0
    pos = np.arange(T)
    inv = (np.float32(10000.0) ** (-np.arange(0, axis, 2, dtype=np.float32) / np.float32(axis))).astype(np.float32)
    ang = np.stack([np.outer((pos // 64).astype(np.float32), inv), np.outer((pos % 64).astype(np.float32), inv)])
    ang = np.repeat(ang[:, None], 2, axis=1).transpose(0, 1, 3, 2).reshape(ROPE, T).astype(np.float32)
    cs = np.stack([np.cos(ang), np.sin(ang)], axis=1).astype(np.float32)
    cnt = np.stack([1.0 / (np.clip(pos + w - w // 2, 0, T) - np.clip(pos - w // 2, 0, T)) for w in WINDOWS])
    cnt = np.broadcast_to(cnt.astype(np.float32), (P, GROUPS, T))
    return ident, turn, cs, cnt


def kernel(**inputs):
    import concourse.bacc as bacc
    from concourse.bass_utils import run_bass_kernel_spmd

    a = {k: np.asarray(v) for k, v in inputs.items()}
    ident, turn, cs, cnt = constants()
    w_in = a["ab_w_in"][0]
    kv0, pool0 = Q_LORA + KV_LORA, Q_LORA + KV_LORA + ROPE
    cin = tiles(a["c_w_in"][0]).reshape(3, NC, P, D).transpose(1, 0, 2, 3).reshape(3 * NC, P, D)
    arrays = {
        "xT": a["x"][0].T.reshape(NC, P, T).transpose(1, 0, 2),
        "ctxT": a["ctx"][0].T.reshape(NC, P, T).transpose(1, 0, 2),
        "c_rows": np.stack([a["c"][0], a["c_ctx"]]),
        "c_cols": np.stack([a["c"][0], a["c_ctx"]]).reshape(2, NC, P).transpose(2, 1, 0),
        "mod_first": a["mod_w"][0, :, :BY_PE * P].reshape(NC // 2, 2, P, BY_PE // 4, 512).transpose(3, 0, 2, 1, 4)
                      .reshape(BY_PE, P, D),
        "mod_t": a["mod_w"].transpose(0, 2, 1).reshape(LAYERS * ROWS, P, D),
        "mod_b": rows(a["mod_b"], LAYERS * ROWS),
        "norms": np.stack([a["norm_mix"], a["norm_ffn"]]).reshape(2 * LAYERS * NC, P).T.reshape(P, 2, LAYERS, NC),
        "win_t": np.concatenate([tiles(w_in[:, :kv0]), tiles(w_in[:, pool0:])]),
        "wrope": w_in[:, kv0:pool0].reshape(NC, P, ROPE).transpose(1, 0, 2),
        "qa_g": rows(a["q_a_norm"][0], QC),
        "kva_g": rows(a["kv_a_norm"][0], KVC),
        "q_g": a["q_norm"][0][:, None],
        "k_g": a["k_norm"][0][:, None],
        "qb_w": a["q_b_w"][0].reshape(QC, P, -1).transpose(1, 0, 2),
        "kvb_w": a["kv_b_w"][0].reshape(KVC, P, -1).transpose(1, 0, 2),
        "pool_w": a["pool_w"][0].transpose(1, 0, 2),
        "pool_s": rows(a["pool_scale"][0], GROUPS),
        "wout_t": tiles(a["ab_w_out"][0]),
        "cin_t": cin,
        "conv_w": a["c_conv"][0].reshape(3, NC, P).transpose(2, 0, 1),
        "cout_t": tiles(a["c_w_out"][0]),
        "wq_t": np.stack([tiles(a["peer_wq"][i]) for i in range(LAYERS)]),
        "keys_t": a["peer_keys"].transpose(0, 2, 4, 1, 3).reshape(LAYERS, P, HEADS, KEYS),
        "u_t": a["peer_u"].reshape(LAYERS, KEYS, KEYS, NC, P).transpose(0, 1, 4, 3, 2).reshape(LAYERS, KEYS, P, D),
        "v_t": a["peer_v"].reshape(LAYERS, KEYS, P, D),
        "ident_c": ident, "rot_c": turn, "cs_c": cs, "cnt_c": cnt,
    }
    arrays = {k: np.ascontiguousarray(v) for k, v in arrays.items()}
    nc = bacc.Bacc("TRN2", target_bir_lowering=False, num_devices=1,
                   dynamic_dma_scratch_size=1024)
    args = {k: nc.dram_tensor(k, v.shape, F32, kind="ExternalInput").ap() for k, v in arrays.items()}
    args["out"] = nc.dram_tensor("out", (P, NC, T), F32, kind="ExternalOutput").ap()
    hybrid_kernel(nc, **args)
    got = run_bass_kernel_spmd(nc, [arrays], core_ids=[0]).results[0]["out"]
    return got.transpose(2, 1, 0).reshape(1, T, D)
```
